# Optimizing a Trainium2 kernel written in Bass

```python
import math, functools
import jax, jax.numpy as jnp
from jax import lax
import numpy as np

D_MODEL = 1024
BATCH = 1
SEQ = 128
DEPTH = 2
DEC_BATCH = 1
DEC_SEQ = 128
PAST_LEN = 128

GRID_W = 64
D_RWKV = 512
RWKV_HEAD = 64
N_RWKV_HEADS = D_RWKV // RWKV_HEAD
LORA_W = 64
LORA_A = 64
LORA_G = 128
RWKV_COLS = (D_RWKV, D_RWKV, D_RWKV, LORA_W, LORA_W, LORA_A, LORA_A, LORA_G)
D_RWKV_PROJ = 3 * D_RWKV + 2 * LORA_W + 2 * LORA_A + LORA_G
DECAY_SCALE = math.exp(-0.5)
GN_EPS = 64e-5
D_HYENA = 512
HYENA_ORDER = 2
HYENA_EMB = 33
HYENA_BANDS = (HYENA_EMB - 1) // 2
HYENA_HIDDEN = 64
HYENA_SHORT = 3
HYENA_FAST_DECAY = 0.3
HYENA_SLOW_DECAY = 1.5
HYENA_TARGET = 1e-2
D_HYENA_PROJ = (HYENA_ORDER + 1) * D_HYENA
N_BRANCH = 2
D_IN_PROJ = D_RWKV_PROJ + D_HYENA_PROJ + N_BRANCH * D_MODEL
D_FF = 2816
N_EXPERTS = 8
TOP_K = 2
D_FF_EXPERT = 1408
N_DENSE = (DEPTH + 1) // 2
N_MOE = DEPTH // 2
N_MOD = 6
DEEPNORM_ALPHA = (2 * DEPTH) ** 0.25
DEEPNORM_BETA = (8 * DEPTH) ** -0.25
LN_EPS = 1e-5
POS_BASE = 10000.0
N_KEYS = 48

kernel_name = 'hybrid_rwkv7_hyena_dit_step'

def _layer_norm(x, g, b):
    xf = x.astype(jnp.float32)
    mean = jnp.mean(xf, axis=-1, keepdims=True)
    var = jnp.mean(jnp.square(xf - mean), axis=-1, keepdims=True)
    return ((xf - mean) * lax.rsqrt(var + LN_EPS)).astype(x.dtype) * g + b

def _prev(x):
    return jnp.pad(x, ((0, 0), (1, 0), (0, 0)))[:, :-1]

def _next(x):
    return jnp.pad(x, ((0, 0), (0, 1), (0, 0)))[:, 1:]

def _split_cols(x, sizes):
    out, start = [], 0
    for s in sizes:
        out.append(x[..., start:start + s])
        start += s
    return out

def _heads(t):
    return t.reshape(t.shape[:-1] + (N_RWKV_HEADS, RWKV_HEAD))

def _adaln(cond, w, b):
    return jax.nn.silu(cond) @ w + b

def _grid_pos_embed(n_tokens, dtype):
    rows = n_tokens // GRID_W
    row = jnp.repeat(jnp.arange(rows, dtype=jnp.float32), GRID_W)
    col = jnp.tile(jnp.arange(GRID_W, dtype=jnp.float32), rows)
    quarter = D_MODEL // 4
    omega = 1.0 / (POS_BASE ** (jnp.arange(quarter, dtype=jnp.float32) / quarter))

    def enc(pos):
        ang = pos[:, None] * omega
        return jnp.concatenate([jnp.sin(ang), jnp.cos(ang)], axis=-1)

    return jnp.concatenate([enc(row), enc(col)], axis=-1).astype(dtype)

def _wkv_scan(r, w, k, v, kk, a, s0, reverse):
    def step(s, inp):
        r_t, w_t, k_t, v_t, kk_t, a_t = inp
        sa = jnp.einsum('bhvk,bhk->bhv', s, -kk_t)
        s = (s * w_t[:, :, None, :] + sa[..., :, None] * (kk_t * a_t)[..., None, :]
             + v_t[..., :, None] * k_t[..., None, :])
        return s, jnp.einsum('bhvk,bhk->bhv', s, r_t)

    xs = tuple(jnp.moveaxis(t.astype(jnp.float32), 1, 0) for t in (r, w, k, v, kk, a))
    s_fin, y = lax.scan(step, s0.astype(jnp.float32), xs, reverse=reverse)
    return jnp.moveaxis(y, 0, 1).astype(r.dtype), s_fin.astype(s0.dtype)

def _rwkv7(p, lp, s0):
    B, L, _ = p.shape
    r, k, v, w_f, w_b, a_f, a_b, g_low = _split_cols(p, RWKV_COLS)
    kk = _heads(k * lp['rwkv_k_k']).astype(jnp.float32)
    kk = (kk * lax.rsqrt(jnp.maximum(jnp.sum(kk * kk, axis=-1, keepdims=True), 1e-24))).astype(p.dtype)
    r_h, v_h = _heads(r), _heads(v)
    ys, ks, finals = [], [], []
    for d, (w_low, a_low) in enumerate(((w_f, a_f), (w_b, a_b))):
        log_w = -DECAY_SCALE * jax.nn.sigmoid(lp['rwkv_w0'][d] + jnp.tanh(w_low) @ lp['rwkv_w2'][d])
        decay = jnp.exp(log_w.astype(jnp.float32))
        a = jax.nn.sigmoid(lp['rwkv_a0'][d] + a_low @ lp['rwkv_a2'][d])
        k_d = _heads(k * (1 + (a - 1) * lp['rwkv_k_a']))
        y_d, s_d = _wkv_scan(r_h, _heads(decay), k_d, v_h, kk, _heads(a), s0[:, d], reverse=(d == 1))
        ys.append(y_d)
        ks.append(k_d)
        finals.append(s_d)
    y32 = (ys[0] + ys[1]).astype(jnp.float32)
    mean = jnp.mean(y32, axis=-1, keepdims=True)
    var = jnp.mean(jnp.square(y32 - mean), axis=-1, keepdims=True)
    y_n = ((y32 - mean) * lax.rsqrt(var + GN_EPS)).astype(p.dtype).reshape(B, L, D_RWKV)
    y_n = y_n * lp['rwkv_gn_w'] + lp['rwkv_gn_b']
    bonus = jnp.sum(r_h * (0.5 * (ks[0] + ks[1])) * lp['rwkv_r_k'], axis=-1, keepdims=True) * v_h
    g = jax.nn.sigmoid(g_low) @ lp['rwkv_g2']
    y = (y_n + bonus.reshape(B, L, D_RWKV)) * g
    return y, jnp.stack(finals, axis=1)

def _hyena_filters(L, lp, dtype):
    t = jnp.linspace(0.0, 1.0, L, dtype=jnp.float32)[:, None]
    f = jnp.linspace(1e-4, HYENA_BANDS - 1, HYENA_BANDS, dtype=jnp.float32)
    ang = (2.0 * math.pi / L) * jnp.arange(L, dtype=jnp.float32)[:, None] * f
    feats = jnp.concatenate([t, jnp.cos(ang), -jnp.sin(ang)], axis=-1).astype(dtype)
    hid = jnp.sin(feats @ lp['hy_f1'] + lp['hy_fb1'])
    hid = jnp.sin(hid @ lp['hy_f2'] + lp['hy_fb2'])
    h = (hid @ lp['hy_f3']).astype(jnp.float32).reshape(L, HYENA_ORDER, 2, D_HYENA)
    deltas = jnp.abs(jnp.linspace(math.log(HYENA_TARGET) / HYENA_SLOW_DECAY,
                                  math.log(HYENA_TARGET) / HYENA_FAST_DECAY, D_HYENA, dtype=jnp.float32))
    h = h * jnp.exp(-t * deltas)[:, None, None, :]
    h_fwd, h_bwd = h[:, :, 0], h[:, :, 1]
    kern = jnp.concatenate([h_fwd, jnp.zeros((1, HYENA_ORDER, D_HYENA), jnp.float32), h_bwd[:0:-1]], axis=0)
    return jnp.fft.rfft(kern, axis=0)

def _hyena(p, lp):
    B, L, _ = p.shape
    cw = lp['hy_conv_w']
    u = cw[0] * _prev(p) + cw[1] * p + cw[2] * _next(p) + lp['hy_conv_b']
    z, *gates = jnp.split(u, HYENA_ORDER + 1, axis=-1)
    kf = _hyena_filters(L, lp, p.dtype)
    for n in range(HYENA_ORDER):
        zf = jnp.fft.rfft(z.astype(jnp.float32), n=2 * L, axis=1)
        conv = jnp.fft.irfft(zf * kf[None, :, n], n=2 * L, axis=1)[:, :L].astype(p.dtype)
        z = gates[n] * (conv + lp['hy_skip'][n] * z)
    return z

def _mixer(h, lp, s0):
    proj = h @ lp['w_in']
    p_r = proj[..., :D_RWKV_PROJ]
    p_h = proj[..., D_RWKV_PROJ:D_RWKV_PROJ + D_HYENA_PROJ]
    g_a, g_b = jnp.split(proj[..., D_RWKV_PROJ + D_HYENA_PROJ:], N_BRANCH, axis=-1)
    mu = lp['rwkv_mu']
    p_r = p_r + mu[0] * (_prev(p_r) - p_r) + mu[1] * (_next(p_r) - p_r)
    y_a, s_fin = _rwkv7(p_r, lp, s0)
    y_b = _hyena(p_h, lp)
    merged = jax.nn.sigmoid(g_a) * (y_a @ lp['w_pa']) + jax.nn.sigmoid(g_b) * (y_b @ lp['w_pb'])
    return merged @ lp['w_o'], s_fin

def _dense_swiglu(h, w_in, w_out):
    gate, up = jnp.split(h @ w_in, 2, axis=-1)
    return (jax.nn.silu(gate) * up) @ w_out

def _moe_swiglu(h, router_w, router_b, w_in, w_out):
    probs = jax.nn.softmax((h @ router_w + router_b).astype(jnp.float32), axis=-1)
    top_p, top_i = lax.top_k(probs, TOP_K)
    top_p = top_p / jnp.sum(top_p, axis=-1, keepdims=True)
    combine = jnp.sum(jax.nn.one_hot(top_i, N_EXPERTS, dtype=jnp.float32) * top_p[..., None], axis=-2)
    gate, up = jnp.split(jnp.einsum('bld,edf->blef', h, w_in), 2, axis=-1)
    act = jax.nn.silu(gate) * up * combine.astype(h.dtype)[..., None]
    return jnp.einsum('blef,efd->bld', act, w_out)

def _block(x, mod, s0, lp, ffn):
    shift1, scale1, gate1, shift2, scale2, gate2 = jnp.split(mod[:, None, :], N_MOD, axis=-1)
    m, s_fin = _mixer(x * (1 + scale1) + shift1, lp, s0)
    x = _layer_norm(DEEPNORM_ALPHA * x + gate1 * m, lp['ln_g'][0], lp['ln_b'][0])
    f = ffn(x * (1 + scale2) + shift2)
    x = _layer_norm(DEEPNORM_ALPHA * x + gate2 * f, lp['ln_g'][1], lp['ln_b'][1])
    return x, s_fin

def setup_inputs(seed: int = 0) -> dict:
    key = jax.random.key(seed)
    keys = jax.random.split(key, N_KEYS)
    it = iter([keys[i] for i in range(N_KEYS)])

    def nrm(shape, scale):
        return jax.random.normal(next(it), shape, jnp.float32) * scale

    def unif(shape, lo, hi):
        return jax.random.uniform(next(it), shape, jnp.float32, lo, hi)

    d, H, N = D_MODEL, N_RWKV_HEADS, RWKV_HEAD
    return {
        'x_prompt': nrm((BATCH, SEQ, d), 1.0),
        'x_sample': nrm((DEC_BATCH, DEC_SEQ, d), 1.0),
        'c': nrm((DEC_BATCH, d), 1.0),
        'state_wkv': nrm((DEC_BATCH, DEPTH, 2, H, N, N), 0.5),
        'c_ctx': nrm((d,), 1.0),
        'w_ada': nrm((DEPTH, d, N_MOD * d), 0.5 * d ** -0.5),
        'b_ada': nrm((DEPTH, N_MOD * d), 0.02),
        'w_in': nrm((DEPTH, d, D_IN_PROJ), d ** -0.5),
        'rwkv_mu': unif((DEPTH, 2, D_RWKV_PROJ), 0.0, 0.5),
        'rwkv_w0': nrm((DEPTH, 2, D_RWKV), 1.0),
        'rwkv_w2': nrm((DEPTH, 2, LORA_W, D_RWKV), LORA_W ** -0.5),
        'rwkv_a0': nrm((DEPTH, 2, D_RWKV), 0.5),
        'rwkv_a2': nrm((DEPTH, 2, LORA_A, D_RWKV), LORA_A ** -0.5),
        'rwkv_g2': nrm((DEPTH, LORA_G, D_RWKV), LORA_G ** -0.5),
        'rwkv_k_k': 0.85 + nrm((DEPTH, D_RWKV), 0.05),
        'rwkv_k_a': 1.0 + nrm((DEPTH, D_RWKV), 0.05),
        'rwkv_r_k': nrm((DEPTH, H, N), 0.1),
        'rwkv_gn_w': 1.0 + nrm((DEPTH, D_RWKV), 0.05),
        'rwkv_gn_b': nrm((DEPTH, D_RWKV), 0.01),
        'hy_conv_w': nrm((DEPTH, HYENA_SHORT, D_HYENA_PROJ), HYENA_SHORT ** -0.5),
        'hy_conv_b': nrm((DEPTH, D_HYENA_PROJ), 0.01),
        'hy_f1': nrm((DEPTH, HYENA_EMB, HYENA_HIDDEN), 2.0 * HYENA_EMB ** -0.5),
        'hy_fb1': nrm((DEPTH, HYENA_HIDDEN), 0.1),
        'hy_f2': nrm((DEPTH, HYENA_HIDDEN, HYENA_HIDDEN), 2.0 * HYENA_HIDDEN ** -0.5),
        'hy_fb2': nrm((DEPTH, HYENA_HIDDEN), 0.1),
        'hy_f3': nrm((DEPTH, HYENA_HIDDEN, HYENA_ORDER * 2 * D_HYENA), 0.1 * HYENA_HIDDEN ** -0.5),
        'hy_skip': nrm((DEPTH, HYENA_ORDER, D_HYENA), 1.0),
        'w_pa': nrm((DEPTH, D_RWKV, d), D_RWKV ** -0.5),
        'w_pb': nrm((DEPTH, D_HYENA, d), D_HYENA ** -0.5),
        'w_o': nrm((DEPTH, d, d), DEEPNORM_BETA * d ** -0.5),
        'ln_g': 1.0 + nrm((DEPTH, 2, d), 0.05),
        'ln_b': nrm((DEPTH, 2, d), 0.01),
        'ffn_w_in': nrm((N_DENSE, d, 2 * D_FF), d ** -0.5),
        'ffn_w_out': nrm((N_DENSE, D_FF, d), DEEPNORM_BETA * D_FF ** -0.5),
        'router_w': nrm((N_MOE, d, N_EXPERTS), d ** -0.5),
        'router_b': nrm((N_MOE, N_EXPERTS), 0.01),
        'exp_w_in': nrm((N_MOE, N_EXPERTS, d, 2 * D_FF_EXPERT), d ** -0.5),
        'exp_w_out': nrm((N_MOE, N_EXPERTS, D_FF_EXPERT, d), DEEPNORM_BETA * D_FF_EXPERT ** -0.5),
    }

def reference(x_prompt, x_sample, c, state_wkv, c_ctx, w_ada, b_ada, w_in, rwkv_mu, rwkv_w0, rwkv_w2,
              rwkv_a0, rwkv_a2, rwkv_g2, rwkv_k_k, rwkv_k_a, rwkv_r_k, rwkv_gn_w, rwkv_gn_b, hy_conv_w,
              hy_conv_b, hy_f1, hy_fb1, hy_f2, hy_fb2, hy_f3, hy_skip, w_pa, w_pb, w_o, ln_g, ln_b,
              ffn_w_in, ffn_w_out, router_w, router_b, exp_w_in, exp_w_out):
    xp = x_prompt
    xs = x_sample + _grid_pos_embed(x_sample.shape[1], x_sample.dtype)[None]
    s0_ctx = jnp.zeros((x_prompt.shape[0], 2, N_RWKV_HEADS, RWKV_HEAD, RWKV_HEAD), state_wkv.dtype)
    ctx_states = []
    for l in range(DEPTH):
        lp = {
            'w_in': w_in[l], 'rwkv_mu': rwkv_mu[l], 'rwkv_w0': rwkv_w0[l], 'rwkv_w2': rwkv_w2[l],
            'rwkv_a0': rwkv_a0[l], 'rwkv_a2': rwkv_a2[l], 'rwkv_g2': rwkv_g2[l], 'rwkv_k_k': rwkv_k_k[l],
            'rwkv_k_a': rwkv_k_a[l], 'rwkv_r_k': rwkv_r_k[l], 'rwkv_gn_w': rwkv_gn_w[l],
            'rwkv_gn_b': rwkv_gn_b[l], 'hy_conv_w': hy_conv_w[l], 'hy_conv_b': hy_conv_b[l],
            'hy_f1': hy_f1[l], 'hy_fb1': hy_fb1[l], 'hy_f2': hy_f2[l], 'hy_fb2': hy_fb2[l],
            'hy_f3': hy_f3[l], 'hy_skip': hy_skip[l], 'w_pa': w_pa[l], 'w_pb': w_pb[l], 'w_o': w_o[l],
            'ln_g': ln_g[l], 'ln_b': ln_b[l],
        }
        if l % 2 == 0:
            ffn = functools.partial(_dense_swiglu, w_in=ffn_w_in[l // 2], w_out=ffn_w_out[l // 2])
        else:
            ffn = functools.partial(_moe_swiglu, router_w=router_w[l // 2], router_b=router_b[l // 2],
                                    w_in=exp_w_in[l // 2], w_out=exp_w_out[l // 2])
        mod_ctx = _adaln(c_ctx[None], w_ada[l], b_ada[l])
        mod_lat = _adaln(c, w_ada[l], b_ada[l])
        xp, s_ctx = _block(xp, mod_ctx, s0_ctx, lp, ffn)
        xs, _ = _block(xs, mod_lat, state_wkv[:, l], lp, ffn)
        ctx_states.append(s_ctx)
    new_state_wkv = jnp.stack(ctx_states, axis=1)
    return (xp, xs, new_state_wkv)


_drawn_inputs = setup_inputs


def setup_inputs(seed=0):
    import zlib

    import numpy as np

    out = dict(_drawn_inputs(seed))
    spreads = {}
    factors = {'state_wkv': 8.0,
     'rwkv_r_k': 2.696,
     'rwkv_gn_w': 24.582,
     'rwkv_gn_b': 64.0,
     'hy_conv_b': 23.944,
     'hy_fb1': 5.934,
     'hy_fb2': 5.601,
     'router_b': 33.421}
    for name, (base, spread) in spreads.items():
        noise = np.random.default_rng([zlib.crc32(name.encode()), seed]).standard_normal(out[name].shape)
        drawn = base * np.exp(spread * noise) if base else spread * noise
        out[name] = __import__('jax').numpy.asarray(drawn.astype(out[name].dtype))
    for name, factor in factors.items():
        out[name] = (out[name] * factor).astype(out[name].dtype)
    return out
```

```python
import math
from contextlib import ExitStack

import numpy as np

import concourse.bass as bass
from concourse import mybir

F32 = mybir.dt.float32
F32R = mybir.dt.float32r
U8 = mybir.dt.uint8
ALU = mybir.AluOpType
ACT = mybir.ActivationFunctionType
AX = mybir.AxisListType

P = 128
D = 1024
KB = D // P
T = 128
G = 2
TOK = G * T
LAYERS = 2
DR = 512
NH, HD = 8, 64
RB = 15
HB = 12
GB = 16
D_IN = (RB + HB + GB) * P
DECAY_SCALE = math.exp(-0.5)
GN_EPS = 64e-5
LN_EPS = 1e-5
ALPHA = (2 * LAYERS) ** 0.25
D_FF = 2816
FF_E = 1408
NE = 8
EMB, HID = 33, 64
RING = 5
TILE = 2048
LEVELS = 6

ROWS = [("mu0", RB), ("cw0", HB), ("mu1", RB), ("cw2", HB), ("cw1", HB), ("cb", HB), ("a0", 8), ("kk", 4), ("ka", 4),
        ("rk", 4), ("gw", 4), ("gb", 4), ("sk", 8)]
ROW_AT, NROW = {}, 0
for _name, _n in ROWS:
    ROW_AT[_name] = NROW
    NROW += _n


def shape_constants():
    i = np.arange(P)
    s, t = i[:, None], i[None, :]
    j = np.arange(T + 1)[None, :]
    tri = np.stack([(s < j) * 1.0 - (s < T // 2), (s >= j) * 1.0 - (s >= T // 2)], 1)
    ang = 2 * np.pi * (s * t % 256) / 256
    nyq = (-1.0) ** i
    cos_a, sin_a = np.cos(ang), np.sin(ang)
    cos_b, sin_b = cos_a.copy(), -sin_a
    cos_b[:, 0] = nyq
    sin_b = sin_b.copy()
    sin_b[:, 0] = nyq
    inv_c, inv_s = 2 * cos_a / 256, -2 * sin_a / 256
    inv_c[0, :] = 1 / 256
    inv_s[0, :] = nyq / 256
    dft = np.stack([cos_a, cos_b, sin_a, sin_b, inv_c, inv_s], 1)
    masks = np.zeros((P, 2, 4, P))
    for d, (strict, incl) in enumerate((((s < t), (s <= t)), ((s > t), (s >= t)))):
        for m, w in enumerate((strict, incl, strict, incl)):
            masks[:, d, m] = w
    level = np.zeros((P, 2, LEVELS, P))
    for lv in range(LEVELS):
        h = 1 << lv
        same = s // (2 * h) == t // (2 * h)
        level[:, 0, lv] = same & ((s // h) % 2 == 0) & ((t // h) % 2 == 1)
        level[:, 1, lv] = same & ((s // h) % 2 == 1) & ((t // h) % 2 == 0)
    lin = np.linspace(0.0, 1.0, T, dtype=np.float32)
    f = np.linspace(1e-4, 15, 16, dtype=np.float32)
    a = np.float32(2 * math.pi / T) * np.arange(T, dtype=np.float32)[:, None] * f
    feats = np.concatenate([lin[:, None], np.cos(a), -np.sin(a)], 1)
    deltas = np.abs(np.linspace(math.log(1e-2) / 1.5, math.log(1e-2) / 0.3, DR, dtype=np.float32))
    window = np.exp(-lin[:, None] * deltas)
    window_b = window.copy()
    window_b[0] = 0
    omega = 1.0 / (10000.0 ** (np.arange(256, dtype=np.float32) / 256))
    enc = lambda pos: np.concatenate([np.sin(pos[:, None] * omega), np.cos(pos[:, None] * omega)], -1)
    pos = np.concatenate([enc((i // 64).astype(np.float32)), enc((i % 64).astype(np.float32))], -1)
    head = (s // HD == t // HD) * 1.0
    gsel = np.zeros((3, G, P))
    gsel[0, 0] = gsel[1, 1] = gsel[2] = 1
    f4 = lambda x: np.ascontiguousarray(x, dtype=np.float32)
    return {"c_ident": f4(np.eye(P)), "c_tri": f4(tri), "c_dft": f4(dft), "c_masks": f4(masks), "c_level": f4(level),
            "c_feats": f4(feats.T), "c_window": f4(np.stack([window, window_b], 1)), "c_pos": f4(pos),
            "c_head": f4(np.stack([head, head / HD], 1)), "c_gsel": f4(gsel),
            "c_rank": f4(np.broadcast_to(NE - np.arange(NE), (P, NE)))}


def tile_list():
    tiles = []
    for l in range(LAYERS):
        tiles += [("ada", l, j, 0) for j in range(24)]
        tiles += [("in", l, i, 0) for i in range(22)]
        tiles += [(k, l, i, 0) for i in range(2) for k in ("pa", "pb")]
        tiles += [("o", l, i, 0) for i in range(4)]
        if l % 2 == 0:
            tiles += [(k, l, i, 0) for i in range(11) for k in ("gate", "up")]
            tiles += [("down", l, i, 0) for i in range(11)]
        else:
            for e in range(NE):
                tiles += [(k, l, i, e) for i in range(6) for k in ("gate", "up")]
                tiles += [("down", l, i, e) for i in range(6)]
    return tiles


def in_blocks(i):
    if i < 7:
        return [2 * i, 2 * i + 1]
    if i == 7:
        return [14]
    return [RB + 2 * (i - 8), RB + 2 * (i - 8) + 1]


class Steps:

    def __init__(self, engine, own):
        self.engine, self.own, self.count, self.also = engine, own, 0, []

    def __call__(self, instruction):
        self.count += 1
        instruction.then_inc(self.own, 1)

    def wait_for(self, other, value):
        self.also.append((other, value))

    def wait(self):
        if self.count:
            self.engine.wait_ge(self.own, self.count)
        for other, value in self.also:
            self.engine.wait_ge(other, value)
        self.also = []


def build(nc, A, y_prompt, y_sample, new_state):
    ctx = ExitStack()
    with ctx:
        cursor = [16512]

        def sb(name, shape, dt=F32, at=None):
            size = int(np.prod(shape[1:])) * (1 if dt == U8 else 4)
            size = (size + 31) // 32 * 32
            if at is None:
                at = cursor[0]
                cursor[0] += size
            return nc.alloc_sbuf_tensor_at(name, shape, dt, offset=at)

        def sem(name):
            return ctx.enter_context(nc.semaphore(name))

        X = sb("X", [P, G, D])
        hth_at = cursor[0]
        HTH = sb("HTH", [P, KB, TOK], F32R)
        HTL = sb("HTL", [P, KB, TOK], F32R)
        MGH = sb("MGH", [P, KB, TOK], F32R, at=hth_at)
        MGL = sb("MGL", [P, KB, TOK], F32R, at=hth_at + KB * TOK * 4)
        GROW = sb("GROW", [33, 2, D])
        W0 = GROW[32:33, 0, :]
        IDENT = sb("IDENT", [P, P])
        TRI = sb("TRI", [P, 2, T + 1])
        DFT = sb("DFT", [P, 6, P])
        MASKS = sb("MASKS", [P, 2, 4, P], U8)
        LEVEL = sb("LEVEL", [P, 2, LEVELS, P], U8)
        HEAD = sb("HEAD", [P, 2, P])
        FEATS = sb("FEATS", [EMB, T])
        GSEL = sb("GSEL", [3, G, P])
        ONES = sb("ONES", [33, P])
        RANK = sb("RANK", [P, NE])
        PROW = sb("PROW", [NROW, P])
        BROW = sb("BROW", [48, P])
        PT = sb("PT", [P, NROW])
        CEN = sb("CEN", [P, RB])
        KAM = sb("KAM", [P, 4])
        KAM2 = sb("KAM2", [P, 4])
        BADT = sb("BADT", [P, 48])
        MODT = sb("MODT", [P, 48, 2])
        COND = sb("COND", [16, P])
        CONDT = sb("CONDT", [P, 16])
        AROW = sb("AROW", [2, 2, 256])
        W2 = sb("W2", [P, DR])
        A2 = sb("A2", [P, DR])
        G2 = sb("G2", [P, DR])
        F1 = sb("F1", [EMB, HID])
        F2 = sb("F2", [HID, HID])
        FB = sb("FB", [HID, 2])
        RW_ = sb("RW_", [P, KB, NE])
        RWH = sb("RWH", [P, KB, NE], F32R)
        RWL = sb("RWL", [P, KB, NE], F32R)
        RBIAS = sb("RBIAS", [1, NE])
        STAT = sb("STAT", [P, 2, 12])
        MV = sb("MV", [P, 2, 4])
        WRING = sb("WRING", [P, RING, TILE])
        WH = sb("WH", [P, 2, TILE], F32R)
        WL = sb("WL", [P, 2, TILE], F32R)
        base = cursor[0]
        room = 229344 - base

        def at(start, name, shape, dt=F32):
            size = int(np.prod(shape[1:])) * 4
            assert start * 4 + size <= room, (name, start * 4 + size, room)
            return sb(name, shape, dt, at=base + start * 4)

        RW = at(0, "RW", [P, RB, TOK])
        SGW = at(3840, "SGW", [P, 4, DR])
        VT = at(5888, "VT", [P, G, DR])
        KK = at(6912, "KK", [P, 4, TOK])
        YT = at(7936, "YT", [P, 4, TOK])
        KS = at(8960, "KS", [P, 4, TOK])
        WLOW = at(9984, "WLOW", [P, TOK])
        GLOW = at(10240, "GLOW", [P, TOK])
        S0R = at(10496, "S0R", [HD, 2, NH, HD])
        S0T = at(11520, "S0T", [P, 8, HD])
        EX = at(12032, "EX", [P, G, T + 1])
        EI = at(12304, "EI", [P, G, T + 1])
        AA = at(12576, "AA", [P, TOK])
        AR = at(12832, "AR", [P, G, 2, T])
        BK = at(13344, "BK", [P, 2, G, T])
        T1 = at(13856, "T1", [P, TOK])
        T2 = at(14112, "T2", [P, TOK])
        MAT = at(14368, "MAT", [P, 4, 4, T])
        AS = at(16416, "AS", [P, 4, T])
        GM = at(16928, "GM", [P, 4, T])
        DM = at(17440, "DM", [P, 4, T])
        XS = at(17952, "XS", [P, 4, T])
        RS = at(18464, "RS", [P, 4, HD])
        UU = at(18720, "UU", [P, 4, HD])
        BKE = at(18976, "BKE", [P, 2, T])
        BKT = at(19232, "BKT", [P, 2, T])
        S0S = at(19488, "S0S", [P, HD])
        SFS = at(19552, "SFS", [HD, 2, HD])
        TMP = at(14368, "TMP", [P, 4, TOK])
        TMP2 = at(15392, "TMP2", [P, 4, TOK])
        TMP3 = at(16416, "TMP3", [P, 4, TOK])
        YAH = at(18432, "YAH", [P, 4, TOK], F32R)
        YAL = at(19456, "YAL", [P, 4, TOK], F32R)
        HY = at(0, "HY", [P, HB, TOK])
        SG = at(3072, "SG", [P, GB, TOK])
        KF = at(7168, "KF", [P, 2, 3, DR])
        ZT = at(10240, "ZT", [P, G, DR])
        PAB = at(11264, "PAB", [P, G, 2, DR])
        F3 = at(13312, "F3", [HID, 4, DR])
        HS = at(15360, "HS", [P, 4, DR])
        CT1 = at(15360, "CT1", [P, DR])
        CT2 = at(15872, "CT2", [P, DR])
        WINDOW = at(17408, "WINDOW", [P, 2, DR])
        HD1 = at(10240, "HD1", [HID, 2, T])
        HDT = at(10496, "HDT", [HID, 2, T])
        YBH = at(13312, "YBH", [P, 4, TOK], F32R)
        YBL = at(14336, "YBL", [P, 4, TOK], F32R)
        MGT = at(7168, "MGT", [P, 2, TOK])
        MG = at(8192, "MG", [P, KB, TOK])
        AH = at(0, "AH", [P, 22, TOK], F32R)
        AL = at(5632, "AL", [P, 22, TOK], F32R)
        CB = at(11264, "CB", [P, NE, TOK])
        GBC = at(13312, "GBC", [P, G, D])
        LNGB = at(15360, "LNGB", [P, 2, D])
        SL = at(17408, "SL", [P, 2, 2, TOK])
        HTF = at(18432, "HTF", [P, KB, TOK])
        POS = at(13312, "POS", [P, D])
        MASKF = at(0, "MASKF", [P, 2, 4, P])
        LEVELF = at(1024, "LEVELF", [P, 2, LEVELS, P])
        LG = at(10240, "LG", [P, G, NE])
        PR = at(10256, "PR", [P, G, NE])
        OH = at(10272, "OH", [P, G, NE])
        PW = at(10288, "PW", [P, G, NE])
        CMB = at(10304, "CMB", [P, G, NE])
        SM = at(10320, "SM", [P, G, 4])
        CTT = at(10336, "CTT", [NE, TOK])

        PS = ctx.enter_context(nc.psum_tensor("PS", [P, 8, 512], F32))

        tiles = tile_list()
        NT = len(tiles)
        number = {t: n for n, t in enumerate(tiles)}
        split_no, k = [], 0
        for t in tiles:
            split_no.append(k)
            k += t[0] != "ada"
        ring_in = [sem(f"ring_in{i}") for i in range(RING)]
        tile_done = sem("tile_done")
        hi_ready = sem("hi_ready")
        lo_ready = sem("lo_ready")

        def split(n):
            return tiles[n][0] != "ada"

        def tile_width(n):
            kind, l, i, e = tiles[n]
            if kind == "in" and i == 7:
                return (KB, P)
            if kind == "ada" or kind == "in":
                return (KB, 256)
            if kind in ("gate", "up"):
                return (KB, 256 if l % 2 == 0 or i < 5 else P)
            if kind in ("pa", "pb"):
                return (4, 512)
            if kind == "down" and l % 2 == 1 and i == 5:
                return (1, D)
            return (2, D)

        def tile_view(tensor, slot, n):
            k, w = tile_width(n)
            return tensor[:, slot, 0:k * w].rearrange("p (k w) -> p k w", k=k)

        def tile_source(n):
            kind, l, i, e = tiles[n]
            k, w = tile_width(n)
            if kind == "ada":
                src = A["w_ada"][l, :, i * 256:(i + 1) * 256]
            elif kind == "in":
                b = in_blocks(i)[0]
                src = A["w_in"][l, :, b * P:b * P + w]
            elif kind in ("pa", "pb"):
                src = A["w_" + kind][l, :, i * 512:(i + 1) * 512]
            elif kind == "o":
                src = A["w_o"][l, i * 256:(i + 1) * 256, :]
            elif kind in ("gate", "up"):
                half = D_FF if l % 2 == 0 else FF_E
                c = (kind == "up") * half + i * 256
                src = (A["ffn_w_in"][l // 2] if l % 2 == 0 else A["exp_w_in"][l // 2, e])[:, c:c + w]
            else:
                src = (A["ffn_w_out"][l // 2] if l % 2 == 0 else A["exp_w_out"][l // 2, e])[i * 256:i * 256 + k * P, :]
            return src.rearrange("(k p) w -> p k w", p=P)

        reader = []
        for kind, l, i, e in tiles:
            reader.append({"ada": "dve", "in": "act" if i >= 14 else "dve", "gate": "act", "up": "dve"}.get(kind))
        read_no = [sum(r == reader[n] for r in reader[:n + 1]) for n in range(NT)]
        bank_of, last_in_bank = [None] * NT, [None] * NT
        u, held = 0, {}
        for n, (kind, l, i, e) in enumerate(tiles):
            if reader[n]:
                bank_of[n] = u % 2
                last_in_bank[n] = held.get(u % 2)
                held[u % 2] = n
                u += 1
        pairs = [t[1:] for t in tiles if t[0] == "gate"]
        pair_no = {t: u for u, t in enumerate(pairs)}
        hidden_no = {(0, 0): 1, **{(1, e): 2 + e for e in range(NE)}}

        def act_reads_through(l):
            return read_no[max(n for n, t in enumerate(tiles) if t[0] == "gate" and t[1] == l)]

        def dve_reads_through(l):
            return read_no[max(n for n, t in enumerate(tiles) if t[0] == "up" and t[1] == l)]

        act_read = sem("act_read")
        dve_read = sem("dve_read")

        sched = [("cond",), ("barrier",)]
        for l in range(LAYERS):
            sched += [("params", l)]
            sched += [("ada", l, j) for j in range(24)] + [("mod", l), ("barrier",), ("ht", l, 0), ("barrier",)]
            sched += [("in", l, i) for i in range(8)] + [("barrier",), ("wprep", l), ("barrier",)]
            sched += [("batch", l, b) for b in range(8)] + [("barrier",), ("gn", l), ("barrier",)]
            sched += [("in", l, i) for i in range(8, 22)] + [("barrier",), ("filter", l), ("barrier",)]
            for o in range(2):
                sched += [("conv", l, o), ("barrier",)]
            sched += [("merge", l, 0), ("merge", l, 1), ("barrier",), ("o", l), ("norm", l, 0), ("barrier",)]
            sched += [("ht", l, 1), ("barrier",)]
            if l % 2 == 0:
                sched += [("pair", l, i, 0) for i in range(11)] + [("down", l, 0)]
            else:
                sched += [("router", l), ("barrier",)]
                for e in range(NE):
                    sched += [("pair", l, i, e) for i in range(6)] + [("down", l, e)]
            sched += [("norm", l, 1), ("barrier",)]
        barriers, seen = {}, 0
        for at_, item in enumerate(sched):
            barriers[at_] = seen
            seen += item[0] == "barrier"
        first_of = {}
        for at_, item in enumerate(sched):
            first_of.setdefault(item, at_)

        def barrier_after(item):
            return barriers[first_of[item]] + 1

        act_stage = sem("act_stage")
        dve_stage = sem("dve_stage")
        E = {}

        def ev(name):
            if name not in E:
                E[name] = sem(name)
            return E[name]

        const_in = sem("const_in")
        x_in = sem("x_in")
        param_in = sem("param_in")
        lngb_in = sem("lngb_in")
        s0_in = sem("s0_in")
        f3_in = sem("f3_in")
        state_out = sem("state_out")
        y_out = sem("y_out")
        CONSTS = [(IDENT, "c_ident"), (TRI, "c_tri"), (DFT, "c_dft"), (MASKF, "c_masks"), (LEVELF, "c_level"),
                  (HEAD, "c_head"), (FEATS, "c_feats"), (GSEL, "c_gsel"),
                  (RANK, "c_rank"), (POS, "c_pos")]
        NCONST = 16 * (len(CONSTS) + 2)
        NPARAM = 16 * (len(ROWS) + 1 + 2 + 4 + 4 + 2)

        block = ctx.enter_context(nc.Block())

        @block.sync
        def _(sp):
            sp.dma_start(X[:, 0, :], A["x_prompt"][0]).then_inc(x_in, 16)
            sp.dma_start(X[:, 1, :], A["x_sample"][0]).then_inc(x_in, 16)
            for n in range(NT):
                if n >= RING:
                    old = n - RING
                    if split(old):
                        sp.wait_ge(lo_ready, split_no[old] + 1)
                    else:
                        sp.wait_ge(tile_done, old + 1)
                sp.dma_start(tile_view(WRING, n % RING, n), tile_source(n)).then_inc(ring_in[n % RING], 16)
            sp.wait_ge(act_stage, seen)
            sp.wait_ge(dve_stage, seen)
            sp.dma_start(y_prompt[0], X[:, 0, :]).then_inc(y_out, 16)
            sp.dma_start(y_sample[0], X[:, 1, :]).then_inc(y_out, 16)
            sp.wait_ge(y_out, 32)
            sp.wait_ge(state_out, 16 * LAYERS * 8)

        @block.gpsimd
        def _(pool):
            pool.memset(ONES[:, :], 1.0).then_inc(ev("ones_set"), 1)
            for dst, name in CONSTS:
                pool.dma_start(dst[:], A[name]).then_inc(const_in, 16)
            pool.dma_start(COND[0:8, :], A["c_ctx"].rearrange("(k p) -> k p", p=P)).then_inc(const_in, 16)
            pool.dma_start(COND[8:16, :], A["c"][0].rearrange("(k p) -> k p", p=P)).then_inc(const_in, 16)

            def layer_params(l):
                srcs = {"mu0": A["rwkv_mu"][l, 0], "mu1": A["rwkv_mu"][l, 1], "cw0": A["hy_conv_w"][l, 0],
                        "cw1": A["hy_conv_w"][l, 1], "cw2": A["hy_conv_w"][l, 2], "cb": A["hy_conv_b"][l],
                        "a0": A["rwkv_a0"][l].rearrange("d n -> (d n)"), "kk": A["rwkv_k_k"][l],
                        "ka": A["rwkv_k_a"][l], "rk": A["rwkv_r_k"][l].rearrange("h n -> (h n)"),
                        "gw": A["rwkv_gn_w"][l], "gb": A["rwkv_gn_b"][l],
                        "sk": A["hy_skip"][l].rearrange("d n -> (d n)")}
                for name, n in ROWS:
                    pool.dma_start(PROW[ROW_AT[name]:ROW_AT[name] + n, :],
                                   srcs[name].rearrange("(b p) -> b p", p=P)).then_inc(param_in, 16)
                pool.dma_start(BROW[:, :], A["b_ada"][l].rearrange("(b p) -> b p", p=P)).then_inc(param_in, 16)
                for w, j in enumerate((2, 5)):
                    pool.dma_start(GROW[2:3, w, :], A["b_ada"][l:l + 1, j * D:(j + 1) * D]).then_inc(param_in, 16)
                pool.dma_start(W2[:, :], A["rwkv_w2"][l].rearrange("d k n -> (d k) n")).then_inc(param_in, 16)
                pool.dma_start(A2[:, :], A["rwkv_a2"][l].rearrange("d k n -> (d k) n")).then_inc(param_in, 16)
                pool.dma_start(G2[:, :], A["rwkv_g2"][l]).then_inc(param_in, 16)
                pool.dma_start(W0, A["rwkv_w0"][l:l + 1].rearrange("a d n -> a (d n)")).then_inc(param_in, 16)
                pool.dma_start(F1[:, :], A["hy_f1"][l]).then_inc(param_in, 16)
                pool.dma_start(F2[:, :], A["hy_f2"][l]).then_inc(param_in, 16)
                pool.dma_start(FB[:, 0:1], A["hy_fb1"][l].rearrange("(p a) -> p a", a=1)).then_inc(param_in, 16)
                pool.dma_start(FB[:, 1:2], A["hy_fb2"][l].rearrange("(p a) -> p a", a=1)).then_inc(param_in, 16)
                pool.dma_start(RW_[:, :, :], A["router_w"][0].rearrange("(k p) e -> p k e", p=P)).then_inc(param_in, 16)
                pool.dma_start(RBIAS[:, :], A["router_b"]).then_inc(param_in, 16)

            def stage_wait(item):
                pool.wait_ge(act_stage, barrier_after(item))
                pool.wait_ge(dve_stage, barrier_after(item))

            for l in range(LAYERS):
                if l > 0:
                    stage_wait(("norm", l - 1, 1))
                layer_params(l)
                stage_wait(("ht", l, 0))
                pool.dma_start(S0R[:, :, :, :], A["state_wkv"][0, l].rearrange("d h v k -> v d h k"))\
                    .then_inc(s0_in, 16)
                stage_wait(("gn", l))
                pool.dma_start(WINDOW[:, :, :], A["c_window"]).then_inc(f3_in, 16)
                pool.dma_start(F3[:, :, :], A["hy_f3"][l].rearrange("k (o n) -> k o n", n=DR)).then_inc(f3_in, 16)
                for w, item in enumerate((("merge", l, 1), ("norm", l, 0))):
                    stage_wait(item)
                    pool.dma_start(LNGB[:, 0, :], A["ln_g"][l, w:w + 1, :].broadcast_to([P, D])).then_inc(lngb_in, 16)
                    pool.dma_start(LNGB[:, 1, :], A["ln_b"][l, w:w + 1, :].broadcast_to([P, D])).then_inc(lngb_in, 16)

        @block.tensor
        def _(pe):
            mm = pe.matmul

            def ready(n):
                if split(n):
                    pe.wait_ge(hi_ready, split_no[n] + 1)
                    pe.wait_ge(lo_ready, split_no[n] + 1)
                else:
                    pe.wait_ge(ring_in[n % RING], 16 * (n // RING + 1))

            def bank_free(n):
                old = last_in_bank[n]
                if old is not None:
                    pe.wait_ge(act_read if reader[old] == "act" else dve_read, read_no[old])

            def product(n, hi, lo, nk=KB):
                ready(n)
                bank_free(n)
                k, w = tile_width(n)
                h, s = tile_view(WH, split_no[n] % 2, n), tile_view(WL, split_no[n] % 2, n)
                for b in range(w // P):
                    out = PS[:, bank_of[n], b * TOK:(b + 1) * TOK]
                    c = slice(b * P, (b + 1) * P)
                    for kb in range(k):
                        mm(out, h[:, kb, c], hi[:, kb, :], start=kb == 0, stop=False)
                        mm(out, h[:, kb, c], lo[:, kb, :], start=False, stop=False)
                        last = mm(out, s[:, kb, c], hi[:, kb, :], start=False, stop=kb == k - 1)
                last.then_inc(tile_done, 1)

            def cond():
                pe.wait_ge(const_in, NCONST)
                pe.wait_ge(ev("ones_set"), 1)
                pe.transpose(PS[:, 2, 0:16], COND[:, :], IDENT[0:16, 0:16]).then_inc(ev("condT"), 1)

            def fan(l, j):
                pe.wait_ge(ev("ada_row"), l * 24 + j + 1)
                src = GROW[0:2, j // 12, (j % 4) * 256:(j % 4 + 1) * 256] if j // 4 in (2, 5) else AROW[0:2, j % 2, :]
                for b in range(2):
                    o = (2 * j + b) * 2
                    last = mm(PS[:, 2, o:o + 2], src[:, b * P:(b + 1) * P], IDENT[0:2, 0:2], start=True, stop=True)
                last.then_inc(ev("ada_col"), 1)

            def params(l):
                pe.wait_ge(param_in, NPARAM * (l + 1))
                if l == 0:
                    pe.wait_ge(ev("cond_silu"), 1)
                pe.transpose(PS[:, 3, 0:NROW], PROW[:, :], IDENT[0:NROW, 0:NROW])
                pe.transpose(PS[:, 3, 256:304], BROW[:, :], IDENT[0:48, 0:48]).then_inc(ev("paramT"), 1)

            def ada(l, j):
                n = number["ada", l, j, 0]
                ready(n)
                bank_free(n)
                w = tile_view(WRING, n % RING, n)
                for kb in range(KB):
                    last = mm(PS[0:2, bank_of[n], 0:256], CONDT[:, kb::8], w[:, kb, :], start=kb == 0, stop=kb == KB - 1)
                last.then_inc(tile_done, 1)
                if j:
                    fan(l, j - 1)
                if j == 23:
                    fan(l, j)

            def ht(l, w):
                for kb in range(KB):
                    for g in range(G):
                        last = pe.transpose(PS[:, 2 + kb // 2, (kb % 2) * TOK + g * T:(kb % 2) * TOK + (g + 1) * T],
                                            X[:, g, kb * P:(kb + 1) * P], IDENT[:, :])
                    if kb % 2:
                        last.then_inc(ev("xT"), 1)

            def wprep(l):
                pe.wait_ge(ev("wlow"), l + 1)
                for d in range(2):
                    for g in range(G):
                        q = slice(HD * d, HD * d + HD)
                        mm(PS[:, 2 + 2 * d + g, :], WLOW[q, g * T:(g + 1) * T], W2[q, :], start=True, stop=False)
                        last = mm(PS[:, 2 + 2 * d + g, :], ONES[32:33, :], W0[:, d * DR:(d + 1) * DR],
                                  start=False, stop=True)
                        last.then_inc(ev("w_pre"), 1)
                for g in range(G):
                    for b in range(4):
                        last = pe.transpose(PS[:, 6 + g, b * P:(b + 1) * P], RW[:, 8 + b, g * T:(g + 1) * T], IDENT[:, :])
                    last.then_inc(ev("vT"), 1)
                pe.wait_ge(ev("sgw"), 4 * (l + 1))
                pe.wait_ge(ev("kk_sq"), l + 1)
                for b in range(4):
                    last = mm(PS[:, 2 + b // 2, (b % 2) * TOK:(b % 2 + 1) * TOK], HEAD[:, 0, :], TMP[:, b, :],
                              start=True, stop=True)
                last.then_inc(ev("kk_norm"), 1)
                pe.wait_ge(s0_in, 16 * (l + 1))
                for d in range(2):
                    for b in range(4):
                        o = (d * 4 + b) * HD
                        last = pe.transpose(PS[:, 4, o:o + HD],
                                            S0R[:, d, 2 * b:2 * b + 2, :].rearrange("v h k -> v (h k)"),
                                            IDENT[0:HD, 0:HD])
                last.then_inc(ev("s0T"), 1)

            def batch(l, b):
                i, blk, d = l * 8 + b, b // 2, b % 2
                for g in range(G):
                    mm(PS[:, 2, g * 129:(g + 1) * 129], SGW[:, d * 2 + g, blk * P:(blk + 1) * P], TRI[:, d, :],
                       start=True, stop=True)
                q = slice(HD * d, HD * d + HD)
                mm(PS[:, 3, 0:TOK], A2[q, blk * P:(blk + 1) * P], RW[q, 13, :], start=True, stop=True)\
                    .then_inc(ev("decay_sum"), 1)
                pe.wait_ge(ev("factors"), i + 1)
                for hh in range(2):
                    r = slice(HD * hh, HD * hh + HD)
                    for g in range(G):
                        o = PS[:, 2 + 2 * hh + g, :]
                        mm(o[:, 0:256], BK[r, 0, g, :], AR[r, g, :, :].rearrange("p a t -> p (a t)"), start=True, stop=True)
                        mm(o[:, 256:512], BK[r, 1, g, :], AR[r, g, :, :].rearrange("p a t -> p (a t)"),
                           start=True, stop=True)
                        last = mm(PS[:, 6 + hh, g * T:(g + 1) * T], AR[r, g, 0, :], BK[r, 0, g, :], start=True, stop=True)
                last.then_inc(ev("grams"), 1)
                pe.wait_ge(ev("mats"), i + 1)
                for hh in range(2):
                    r = slice(HD * hh, HD * hh + HD)
                    v = slice((2 * blk + hh) * HD, (2 * blk + hh + 1) * HD)
                    mm(PS[:, 2 + hh, HD:2 * HD], AR[r, 1, 0, :], S0S[r, :], start=True, stop=False, skip_group_check=True)
                    for g in range(G):
                        last = mm(PS[:, 2 + hh, g * HD:(g + 1) * HD], MAT[:, 2 * hh + g, 2, :], VT[:, g, v],
                                  start=False, stop=False, skip_group_check=True)
                last.then_inc(ev("rhs"), 1)
                for lv in range(1, LEVELS):
                    n = i * (LEVELS - 1) + lv
                    pe.wait_ge(ev("inverse"), n + i)
                    for s in range(4):
                        last = mm(PS[:, 4, s * T:(s + 1) * T], AS[:, s, :], GM[:, s, :], start=True, stop=True)
                    last.then_inc(ev("cross"), 1)
                    pe.wait_ge(ev("cross_masked"), n)
                    for s in range(4):
                        mm(PS[:, 5, s * T:(s + 1) * T], DM[:, s, :], XS[:, s, :], start=True, stop=True)
                        last = mm(PS[:, 6, s * T:(s + 1) * T], XS[:, s, :], DM[:, s, :], start=True, stop=True)
                    last.then_inc(ev("update"), 1)
                lo, hi = (slice(0, 64), slice(64, 128)) if d == 0 else (slice(64, 128), slice(0, 64))
                pe.wait_ge(ev("inverse"), (i + 1) * LEVELS)
                pe.wait_ge(ev("rhs_lo"), i + 1)
                for s in range(4):
                    last = mm(PS[lo, 4, s * HD:(s + 1) * HD], GM[lo, s, lo], RS[lo, s, :], start=True, stop=True)
                last.then_inc(ev("sa_lo_ps"), 1)
                pe.wait_ge(ev("sa_lo"), i + 1)
                for s in range(4):
                    last = mm(PS[hi, 2 + s // 2, (s % 2) * HD:(s % 2 + 1) * HD], MAT[lo, s, 0, hi], UU[lo, s, :],
                              start=False, stop=False, skip_group_check=True)
                last.then_inc(ev("rhs_hi_ps"), 1)
                pe.wait_ge(ev("rhs_hi"), i + 1)
                for s in range(4):
                    last = mm(PS[hi, 5, s * HD:(s + 1) * HD], GM[hi, s, hi], RS[hi, s, :], start=True, stop=True)
                last.then_inc(ev("sa_hi_ps"), 1)
                pe.wait_ge(ev("sa_hi"), i + 1)
                for hh in range(2):
                    r = slice(HD * hh, HD * hh + HD)
                    v = slice((2 * blk + hh) * HD, (2 * blk + hh + 1) * HD)
                    for g in range(G):
                        s = 2 * hh + g
                        o = PS[r, 6 + hh, g * T:(g + 1) * T]
                        mm(o, UU[:, s, :], MAT[:, s, 1, :], start=g == 0, stop=False, skip_group_check=True)
                        last = mm(o, VT[:, g, v], MAT[:, s, 3, :], start=False, stop=g == 0, skip_group_check=True)
                    last = mm(PS[r, 6 + hh, T:2 * T], S0S[r, :], AR[r, 1, 1, :], start=False, stop=True,
                              skip_group_check=True)
                last.then_inc(ev("y_ps"), 1)
                for x in range(2):
                    last = pe.transpose(PS[:, 4, x * T:(x + 1) * T], BKE[:, x, :], IDENT[:, :])
                last.then_inc(ev("bkT"), 1)
                pe.wait_ge(ev("bk_copied"), i + 1)
                for hh in range(2):
                    v = slice((2 * blk + hh) * HD, (2 * blk + hh + 1) * HD)
                    c = slice(hh * HD, (hh + 1) * HD)
                    mm(PS[0:HD, 5, c], UU[:, 2 * hh, :], BKT[:, 0, c], start=True, stop=False)
                    last = mm(PS[0:HD, 5, c], VT[:, 0, v], BKT[:, 1, c], start=False, stop=True)
                last.then_inc(ev("state_ps"), 1)
                pe.wait_ge(ev("state_copied"), i + 1)
                pe.wait_ge(ev("y_added"), i + 1)

            def head_sums(src, which, bank):
                for b in range(4):
                    last = mm(PS[:, bank + b // 2, (b % 2) * TOK:(b % 2 + 1) * TOK], HEAD[:, which, :], src[:, b, :],
                              start=True, stop=True)
                return last

            def gn(l):
                head_sums(YT, 1, 2).then_inc(ev("gn_mean"), 1)
                for b in range(4):
                    last = mm(PS[:, 6 + b // 2, (b % 2) * TOK:(b % 2 + 1) * TOK], G2[:, b * P:(b + 1) * P], GLOW[:, :],
                              start=True, stop=True)
                last.then_inc(ev("g_ps"), 1)
                pe.wait_ge(ev("gn_sq"), l + 1)
                head_sums(TMP, 1, 4).then_inc(ev("gn_var"), 1)
                pe.wait_ge(ev("rk_prod"), l + 1)
                head_sums(TMP3, 0, 2).then_inc(ev("bonus"), 1)

            def filt(l):
                mm(PS[0:HID, 2, 0:T], F1[:, :], FEATS[:, :], start=True, stop=True).then_inc(ev("hid1_ps"), 1)
                pe.wait_ge(ev("hid1"), l + 1)
                mm(PS[0:HID, 3, 0:T], F2[:, :], HD1[:, 0, :], start=True, stop=True).then_inc(ev("hid2_ps"), 1)
                pe.wait_ge(ev("hid2"), l + 1)
                pe.wait_ge(f3_in, 32 * (l + 1))
                for o in range(4):
                    last = mm(PS[:, 4 + o, :], HD1[:, 1, :], F3[:, o, :], start=True, stop=True)
                last.then_inc(ev("filt_ps"), 1)
                pe.wait_ge(ev("filt"), l + 1)
                for o in range(2):
                    mm(PS[:, 2 + 3 * o, :], DFT[:, 0, :], HS[:, 2 * o, :], start=True, stop=True)
                    mm(PS[:, 3 + 3 * o, :], DFT[:, 1, :], HS[:, 2 * o, :], start=True, stop=True)
                    last = mm(PS[:, 4 + 3 * o, :], DFT[:, 2, :], HS[:, 2 * o + 1, :], start=True, stop=True)
                last.then_inc(ev("spec_ps"), 1)

            def conv(l, o):
                i = l * 2 + o
                for g in range(G):
                    for b in range(4):
                        last = pe.transpose(PS[:, 2 + g, b * P:(b + 1) * P], HY[:, b, g * T:(g + 1) * T], IDENT[:, :])
                last.then_inc(ev("zT_ps"), 1)
                pe.wait_ge(ev("zT"), i + 1)
                for g in range(G):
                    mm(PS[:, 4 + 2 * g, :], DFT[:, 0, :], ZT[:, g, :], start=True, stop=True)
                    mm(PS[:, 5 + 2 * g, :], DFT[:, 3, :], ZT[:, g, :], start=True, stop=True).then_inc(ev("zF"), 1)
                pe.wait_ge(ev("spectrum"), i + 1)
                for b in range(4):
                    for g in range(G):
                        out = PS[:, 2 + b // 2, (b % 2) * TOK + g * T:(b % 2) * TOK + (g + 1) * T]
                        mm(out, PAB[:, g, 0, b * P:(b + 1) * P], DFT[:, 4, :], start=True, stop=False)
                        last = mm(out, PAB[:, g, 1, b * P:(b + 1) * P], DFT[:, 5, :], start=False, stop=True)
                last.then_inc(ev("conv_ps"), 1)

            def merge(l, i):
                for x, (kind, hi, lo) in enumerate((("pa", YAH, YAL), ("pb", YBH, YBL))):
                    n = number[kind, l, i, 0]
                    ready(n)
                    h, s = tile_view(WH, split_no[n] % 2, n), tile_view(WL, split_no[n] % 2, n)
                    for b in range(4):
                        out = PS[:, 4 * i + 2 * x + b // 2, (b % 2) * TOK:(b % 2 + 1) * TOK]
                        c = slice(b * P, (b + 1) * P)
                        for kb in range(4):
                            mm(out, h[:, kb, c], hi[:, kb, :], start=kb == 0, stop=False)
                            mm(out, h[:, kb, c], lo[:, kb, :], start=False, stop=False)
                            last = mm(out, s[:, kb, c], hi[:, kb, :], start=False, stop=kb == 3)
                    last.then_inc(tile_done, 1)

            def accumulate(n, hi, lo, kb0, nk):
                ready(n)
                k, w = tile_width(n)
                h, s = tile_view(WH, split_no[n] % 2, n), tile_view(WL, split_no[n] % 2, n)
                for j in range(k):
                    for g in range(G):
                        t = slice(g * T, (g + 1) * T)
                        for c in range(2):
                            out = PS[:, 4 + 2 * g + c, :]
                            w_ = slice(c * 512, (c + 1) * 512)
                            f, e_ = kb0[0] == 0, kb0[0] == nk - 1
                            mm(out, hi[:, kb0[1], t], h[:, j, w_], start=f, stop=False)
                            mm(out, lo[:, kb0[1], t], h[:, j, w_], start=False, stop=False)
                            last = mm(out, hi[:, kb0[1], t], s[:, j, w_], start=False, stop=e_)
                    kb0[0] += 1
                    kb0[1] += 1
                last.then_inc(tile_done, 1)

            def gate_rows(l, w):
                for g in range(G):
                    for c in range(2):
                        last = mm(PS[:, 2 * g + c, :], GSEL[:, g, :], GROW[0:3, w, c * 512:(c + 1) * 512], start=True, stop=True)
                last.then_inc(ev("gate_ps"), 1)

            def out_proj(l):
                gate_rows(l, 0)
                at_k = [0, 0]
                for i in range(4):
                    accumulate(number["o", l, i, 0], MGH, MGL, at_k, 8)

            def router(l):
                for g in range(G):
                    o = PS[:, 2, g * NE:(g + 1) * NE]
                    mm(o, ONES[0:1, :], RBIAS[0:1, :], start=g == 0, stop=False, skip_group_check=True)
                    for kb in range(KB):
                        t = slice(g * T, (g + 1) * T)
                        mm(o, HTH[:, kb, t], RWH[:, kb, :], start=False, stop=False, skip_group_check=True)
                        mm(o, HTL[:, kb, t], RWH[:, kb, :], start=False, stop=False, skip_group_check=True)
                        last = mm(o, HTH[:, kb, t], RWL[:, kb, :], start=False, stop=kb == KB - 1, skip_group_check=True)
                last.then_inc(ev("logits"), 1)
                pe.wait_ge(ev("combine"), 1)
                for g in range(G):
                    last = pe.transpose(PS[0:NE, 3, g * T:(g + 1) * T], CMB[:, g, :], IDENT[:, :])
                last.then_inc(ev("combT"), 1)
                pe.wait_ge(ev("combT_copied"), 1)
                for e in range(NE):
                    last = mm(PS[:, 4 + e // 2, (e % 2) * TOK:(e % 2 + 1) * TOK], IDENT[0:NE, e:e + 1].broadcast_to([NE, P]), CTT[:, :], start=True, stop=True)
                last.then_inc(ev("comb_ps"), 1)

            acc = [0, 0]
            k_bar = 0
            for item in sched:
                what, a = item[0], item[1:]
                if what == "barrier":
                    k_bar += 1
                    pe.wait_ge(act_stage, k_bar)
                    pe.wait_ge(dve_stage, k_bar)
                elif what == "in":
                    product(number["in", a[0], a[1], 0], HTH, HTL)
                elif what == "pair":
                    l, i, e = a
                    product(number["gate", l, i, e], HTH, HTL)
                    product(number["up", l, i, e], HTH, HTL)
                elif what == "down":
                    l, e = a
                    nk = 22 if l % 2 == 0 else 11
                    total = nk if l % 2 == 0 else nk * NE
                    if e == 0:
                        acc[0] = 0
                    acc[1] = 0 if l % 2 == 0 else 11 * (e % 2)
                    pe.wait_ge(ev("hidden_lo"), hidden_no[l, e])
                    for i in range(nk // 2 + nk % 2):
                        accumulate(number["down", l, i, e], AH, AL, acc, total)
                    if e == (0 if l % 2 == 0 else NE - 1):
                        pe.wait_ge(act_read, act_reads_through(l))
                        pe.wait_ge(dve_read, dve_reads_through(l))
                        gate_rows(l, 1)
                elif what in ("norm", "mod"):
                    pass
                else:
                    {"cond": cond, "params": params, "ada": ada, "ht": ht, "wprep": wprep, "batch": batch, "gn": gn,
                     "filter": filt, "conv": conv, "merge": merge, "o": out_proj, "router": router}[what](*a)

        @block.scalar
        def _(act):
            steps = Steps(act, sem("act_steps"))
            fn = act.activation

            def make_hi(n):
                if n >= NT or not split(n):
                    return
                m = split_no[n]
                act.wait_ge(ring_in[n % RING], 16 * (n // RING + 1))
                if m >= 2:
                    prev = next(q for q in range(n - 1, -1, -1) if split(q) and split_no[q] == m - 2)
                    act.wait_ge(tile_done, prev + 1)
                k, w = tile_width(n)
                fn(WH[:, m % 2, 0:k * w], WRING[:, n % RING, 0:k * w], ACT.Copy).then_inc(hi_ready, 1)

            def cond():
                act.wait_ge(ev("condT"), 1)
                steps(fn(CONDT[:, :], PS[:, 2, 0:16], ACT.Silu))
                steps.wait()
                act.sem_inc(ev("cond_silu"), 1)

            def mod_columns(l, w):
                return 3 * w * 8, (3 * w + 1) * 8

            def ht(l, w):
                shift, scale = mod_columns(l, w)
                for kb in range(KB):
                    act.wait_ge(ev("xT"), (l * 2 + w) * KB // 2 + kb // 2 + 1)
                    for g in range(G):
                        steps(fn(HTF[:, kb, g * T:(g + 1) * T],
                                 PS[:, 2 + kb // 2, (kb % 2) * TOK + g * T:(kb % 2) * TOK + (g + 1) * T],
                                 ACT.Identity, bias=MODT[:, shift + kb, g:g + 1], scale=MODT[:, scale + kb, g:g + 1]))
                for half in range(2):
                    q = slice(4 * half, 4 * half + 4)
                    steps.wait()
                    fn(HTH[:, q, :], HTF[:, q, :], ACT.Copy).then_inc(ev("ht_hi"), 1)
                act.wait_ge(ev("ht_hi"), (l * 2 + w) * 2 + 2)
                if l == 1 and w == 1:
                    steps(fn(RWH[:, :, :], RW_[:, :, :], ACT.Copy))
                    steps.wait()
                    act.sem_inc(ev("router_hi"), 1)

            def mixed(l, i):
                n = number["in", l, i, 0]
                make_hi(n + 1)
                act.wait_ge(tile_done, n + 1)
                for x, b in enumerate(in_blocks(i)):
                    src = PS[:, bank_of[n], x * TOK:(x + 1) * TOK]
                    if b < RB:
                        last = fn(RW[:, b, :], src, ACT.Identity, scale=CEN[:, b:b + 1])
                    elif b < RB + HB:
                        c = b - RB
                        last = fn(HY[:, c, :], src, ACT.Identity, scale=PT[:, ROW_AT["cw1"] + c:ROW_AT["cw1"] + c + 1],
                                  bias=PT[:, ROW_AT["cb"] + c:ROW_AT["cb"] + c + 1])
                    else:
                        last = fn(SG[:, b - RB - HB, :], src, ACT.Sigmoid)
                if i < 14:
                    last.then_inc(ev("center"), 1)
                    steps.wait_for(ev("center"), l * 14 + i + 1)
                else:
                    last.then_inc(act_read, 1)
                    steps.wait_for(act_read, read_no[n])

            def wprep(l):
                fn(WLOW[:, :], RW[:, 12, :], ACT.Tanh).then_inc(ev("wlow"), 1)
                steps(fn(GLOW[:, :], RW[:, 14, :], ACT.Sigmoid))
                for x in range(4):
                    act.wait_ge(ev("w_pre"), l * 4 + x + 1)
                    fn(SGW[:, x, :], PS[:, 2 + x, :], ACT.Sigmoid).then_inc(ev("sgw"), 1)
                for g in range(G):
                    act.wait_ge(ev("vT"), l * 2 + g + 1)
                    steps(fn(VT[:, g, :], PS[:, 6 + g, :], ACT.Copy))
                act.wait_ge(ev("s0T"), l + 1)
                steps(fn(S0T[:, :, :], PS[:, 4, :].rearrange("p (a b) -> p a b", a=8), ACT.Copy))
                act.wait_ge(ev("kk_max"), l + 1)
                fn(TMP2[:, :, :], TMP2[:, :, :], ACT.Sqrt).then_inc(ev("kk_root"), 1)
                act.wait_ge(ev("kk_root"), l + 1)
                act.wait_ge(ev("sgw"), 4 * (l + 1))

            def batch(l, b):
                i, blk, d = l * 8 + b, b // 2, b % 2
                act.wait_ge(ev("decay_sum"), i + 1)
                if i:
                    act.wait_ge(ev("y_ps"), i)
                    act.wait_ge(ev("factors"), i)
                o = PS[:, 2, 0:258].rearrange("p (g t) -> p g t", g=2)
                fn(AA[:, :], PS[:, 3, 0:TOK], ACT.Sigmoid, bias=PT[:, ROW_AT["a0"] + d * 4 + blk:ROW_AT["a0"] + d * 4 + blk + 1])
                fn(EX[:, :, :], o, ACT.Exp, scale=-DECAY_SCALE)
                fn(EI[:, :, :], o, ACT.Exp, scale=DECAY_SCALE).then_inc(ev("decays"), 1)
                act.wait_ge(ev("bkT"), i + 1)
                if i:
                    act.wait_ge(ev("state_ps"), i)
                fn(BKT[:, :, :], PS[:, 4, 0:2 * T].rearrange("p (a t) -> p a t", a=2), ACT.Copy).then_inc(ev("bk_copied"), 1)
                act.wait_ge(ev("state_ps"), i + 1)
                if i:
                    act.wait_ge(state_out, 16 * i)
                fn(SFS[:, :, :], PS[0:HD, 5, 0:P].rearrange("p (a t) -> p a t", a=2), ACT.Copy)\
                    .then_inc(ev("state_copied"), 1)
                act.wait_ge(ev("state_copied"), i + 1)
                act.dma_start(new_state[0, l, d, 2 * blk:2 * blk + 2].rearrange("h v k -> v h k"), SFS[:, :, :])\
                    .then_inc(state_out, 16)

            def gn(l):
                act.wait_ge(ev("gn_cent"), l + 1)
                fn(TMP[:, :, :], YT[:, :, :], ACT.Square).then_inc(ev("gn_sq"), 1)
                act.wait_ge(ev("gn_eps"), l + 1)
                fn(TMP2[:, :, :], TMP2[:, :, :], ACT.Sqrt).then_inc(ev("gn_root"), 1)
                act.wait_ge(ev("ya"), l + 1)
                fn(YAH[:, :, :], YT[:, :, :], ACT.Copy).then_inc(ev("ya_hi"), 1)
                act.wait_ge(ev("ya_hi"), l + 1)

            def filt(l):
                act.wait_ge(ev("arg1"), l + 1)
                fn(HD1[:, 0, :], HDT[:, 0, :], ACT.Sin).then_inc(ev("hid1"), 1)
                act.wait_ge(ev("arg2"), l + 1)
                fn(HD1[:, 1, :], HDT[:, 0, :], ACT.Sin).then_inc(ev("hid2"), 1)
                act.wait_ge(ev("spec_ps"), l + 1)
                steps(fn(KF[:, :, :, :].rearrange("p o c n -> p (o c) n"), PS[:, 2:8, :], ACT.Copy))

            def conv(l, o):
                i = l * 2 + o
                act.wait_ge(ev("zT_ps"), i + 1)
                fn(ZT[:, :, :], PS[:, 2:4, :], ACT.Copy).then_inc(ev("zT"), 1)
                act.wait_ge(ev("zT"), i + 1)
                if o == 1:
                    act.wait_ge(ev("yb"), l + 1)
                    fn(YBH[:, :, :], HY[:, 0:4, :], ACT.Copy).then_inc(ev("yb_hi"), 1)
                    act.wait_ge(ev("yb_hi"), l + 1)

            def merge(l, i):
                make_hi(number["pb", l, i, 0])
                make_hi(number["pb", l, i, 0] + 1)
                act.wait_ge(ev("merged"), 4 * (l * 2 + i) + 4)
                fn(MGH[:, 4 * i:4 * i + 4, :], MG[:, 4 * i:4 * i + 4, :], ACT.Copy).then_inc(ev("mg_hi"), 1)
                act.wait_ge(ev("mg_hi"), l * 2 + i + 1)

            def norm(l, w):
                i = l * 2 + w
                if w == 0:
                    for j in range(4):
                        make_hi(number["o", l, j, 0] + 1)
                else:
                    pass
                act.wait_ge(ev("gate_ps"), i + 1)
                fn(GBC[:, :, :].rearrange("p g (c n) -> p (g c) n", c=2), PS[:, 0:4, :], ACT.Copy).then_inc(ev("gate_rows"), 1)
                for g in range(G):
                    act.wait_ge(ev("var"), i * 2 + g + 1)
                    fn(MV[:, g, 2:3], MV[:, g, 1:2], ACT.Sqrt).then_inc(ev("std"), 1)
                act.wait_ge(ev("std"), i * 2 + 2)
                act.wait_ge(ev("gate_rows"), i + 1)

            def router(l):
                act.wait_ge(ev("shifted"), 1)
                fn(PR[:, :, :], LG[:, :, :], ACT.Exp).then_inc(ev("exps"), 1)
                act.wait_ge(ev("combT"), 1)
                fn(CTT[:, :], PS[0:NE, 3, 0:TOK], ACT.Copy).then_inc(ev("combT_copied"), 1)
                act.wait_ge(ev("comb_ps"), 1)
                steps(fn(CB[:, :, :].rearrange("p (a b) t -> p a (b t)", a=4), PS[:, 4:8, :], ACT.Copy))

            def pair(l, i, e):
                n = number["gate", l, i, e]
                make_hi(n + 1)
                act.wait_ge(tile_done, n + 1)
                u = pair_no[l, i, e]
                k, w = tile_width(n)
                if u >= 2:
                    act.wait_ge(ev("pair_lo"), u - 1)
                fn(SL[:, u % 2, 0:w // P, :], PS[:, bank_of[n], 0:w * 2].rearrange("p (b t) -> p b t", t=TOK), ACT.Silu)\
                    .then_inc(act_read, 1)
                make_hi(n + 2)
                if i == 0 and l % 2 == 1 and e >= 2:
                    act.wait_ge(tile_done, number["down", l, 5, e - 2] + 1)
                act.wait_ge(ev("hidden"), u + 1)
                o = (0 if l % 2 == 0 else 11 * (e % 2)) + 2 * i
                fn(AH[:, o:o + w // P, :], SL[:, u % 2, 0:w // P, :], ACT.Copy).then_inc(ev("pair_hi"), 1)
                act.wait_ge(ev("pair_hi"), u + 1)

            def down(l, e):
                cnt = 11 if l % 2 == 0 else 6
                for i in range(cnt):
                    make_hi(number["down", l, i, e] + 1)

            k_bar = 0
            for item in sched:
                what, a = item[0], item[1:]
                if what == "barrier":
                    k_bar += 1
                    steps.wait()
                    act.sem_inc(act_stage, 1)
                    act.wait_ge(dve_stage, k_bar)
                elif what in ("params", "mod"):
                    pass
                elif what == "ada":
                    if a[1] == 23:
                        make_hi(number["in", a[0], 0, 0])
                elif what == "in":
                    mixed(*a)
                elif what == "o":
                    pass
                else:
                    {"cond": cond, "ht": ht, "wprep": wprep, "batch": batch, "gn": gn, "filter": filt, "conv": conv,
                     "merge": merge, "norm": norm, "router": router, "pair": pair, "down": down}[what](*a)

        @block.vector
        def _(dve):
            steps = Steps(dve, sem("dve_steps"))
            tt, ts, stt = dve.tensor_tensor, dve.tensor_scalar, dve.scalar_tensor_tensor

            def col(name, b):
                return PT[:, ROW_AT[name] + b:ROW_AT[name] + b + 1]

            def make_lo(n):
                if n >= NT or not split(n):
                    return
                m = split_no[n]
                dve.wait_ge(hi_ready, m + 1)
                k, w = tile_width(n)
                tt(WL[:, m % 2, 0:k * w], WRING[:, n % RING, 0:k * w], WH[:, m % 2, 0:k * w].bitcast(F32), ALU.subtract)\
                    .then_inc(lo_ready, 1)

            def cond():
                dve.wait_ge(x_in, 32)
                dve.wait_ge(const_in, NCONST)
                steps(tt(X[:, 1, :], X[:, 1, :], POS[:, :], ALU.add))
                steps(dve.tensor_copy(MASKS[:, :, :, :], MASKF[:, :, :, :]))
                steps(dve.tensor_copy(LEVEL[:, :, :, :], LEVELF[:, :, :, :]))

            def params(l):
                dve.wait_ge(ev("paramT"), l + 1)
                steps(dve.tensor_copy(PT[:, :], PS[:, 3, 0:NROW]))
                steps(dve.tensor_copy(BADT[:, :], PS[:, 3, 256:304]))
                steps.wait()
                steps(tt(CEN[:, :], PT[:, 0:RB], PT[:, ROW_AT["mu1"]:ROW_AT["mu1"] + RB], ALU.add))
                steps(ts(KAM[:, :], PT[:, ROW_AT["ka"]:ROW_AT["ka"] + 4], -1.0, 1.0, ALU.mult, ALU.add))
                steps.wait()
                steps(ts(CEN[:, :], CEN[:, :], -1.0, 1.0, ALU.mult, ALU.add))
                steps(ts(KAM2[:, :], KAM[:, :], 2.0, None, ALU.mult))

            def ada(l, j):
                n = number["ada", l, j, 0]
                i = l * 24 + j
                dve.wait_ge(tile_done, n + 1)
                if i >= 2:
                    dve.wait_ge(ev("ada_col"), i - 1)
                dst = GROW[0:2, j // 12, (j % 4) * 256:(j % 4 + 1) * 256] if j // 4 in (2, 5) else AROW[0:2, j % 2, :]
                dve.tensor_copy(dst, PS[0:2, bank_of[n], 0:256]).then_inc(ev("ada_row"), 1)
                dve.wait_ge(ev("ada_row"), i + 1)
                dve.sem_inc(dve_read, 1)

            def mod(l):
                make_lo(number["in", l, 0, 0])
                dve.wait_ge(ev("ada_col"), 24 * (l + 1))
                bias = BADT[:, :].rearrange("p (b a) -> p b a", a=1).broadcast_to([P, 48, 2])
                steps.wait()
                steps(tt(MODT[:, :, :], PS[:, 2, 0:96].rearrange("p (b c) -> p b c", c=2), bias, ALU.add))
                steps.wait()
                for s in (8, 32):
                    steps(ts(MODT[:, s:s + 8, :], MODT[:, s:s + 8, :], 1.0, None, ALU.add))

            def ht(l, w):
                for half in range(2):
                    q = slice(4 * half, 4 * half + 4)
                    dve.wait_ge(ev("ht_hi"), (l * 2 + w) * 2 + half + 1)
                    steps(tt(HTL[:, q, :], HTF[:, q, :], HTH[:, q, :].bitcast(F32), ALU.subtract))
                if l == 1 and w == 1:
                    dve.wait_ge(ev("router_hi"), 1)
                    steps(tt(RWL[:, :, :], RW_[:, :, :], RWH[:, :, :].bitcast(F32), ALU.subtract))

            def mixed(l, i):
                n = number["in", l, i, 0]
                make_lo(n + 1)
                if i >= 14:
                    return
                dve.wait_ge(ev("center"), l * 14 + i + 1)
                for side in range(2):
                    for x, b in enumerate(in_blocks(i)):
                        src = PS[:, bank_of[n], x * TOK:(x + 1) * TOK].rearrange("p (g t) -> p g t", g=G)
                        dst = RW[:, b, :] if b < RB else HY[:, b - RB, :]
                        dst = dst.rearrange("p (g t) -> p g t", g=G)
                        o, s = (dst[:, :, 1:T], src[:, :, 0:T - 1]) if side == 0 else (dst[:, :, 0:T - 1], src[:, :, 1:T])
                        c = b + side * (RB + HB)
                        last = stt(o, s, PT[:, c:c + 1], o, ALU.mult, ALU.add)
                        if side == 1 and x == len(in_blocks(i)) - 1:
                            last.then_inc(dve_read, 1)
                            steps.wait_for(dve_read, read_no[n])
                        else:
                            steps(last)
                    if side == 0:
                        steps.wait()

            def wprep(l):
                for b in range(4):
                    steps(ts(KK[:, b, :], RW[:, 4 + b, :], col("kk", b), None, ALU.mult))
                steps.wait()
                tt(TMP[:, :, :], KK[:, :, :], KK[:, :, :], ALU.mult).then_inc(ev("kk_sq"), 1)
                dve.wait_ge(ev("kk_norm"), l + 1)
                ts(TMP2[:, :, :].rearrange("p (a b) t -> p a (b t)", a=2), PS[:, 2:4, :], 1e-24, None, ALU.max)\
                    .then_inc(ev("kk_max"), 1)
                dve.wait_ge(ev("kk_root"), l + 1)
                steps(dve.reciprocal(TMP2[:, :, :], TMP2[:, :, :]))
                steps.wait()
                steps(tt(KK[:, :, :], KK[:, :, :], TMP2[:, :, :], ALU.mult))
                steps.wait()

            def batch(l, b):
                i, blk, d = l * 8 + b, b // 2, b % 2
                own, nxt = (1, 0) if d == 0 else (0, 1)
                if b % 2 == 0 or True:
                    steps(dve.memset(MAT[:, :, :, :], 0.0))
                    steps(dve.memset(AS[:, :, :], 0.0))
                dve.wait_ge(ev("decays"), i + 1)
                if i:
                    dve.wait_ge(ev("state_ps"), i)
                E_ = lambda x, o: x[:, :, o:o + T]
                g3 = lambda x: x.rearrange("p (g t) -> p g t", g=G)
                kblk, rblk, kkb = RW[:, 4 + blk, :], RW[:, blk, :], KK[:, blk, :]
                steps(stt(AR[:, :, 0, :], g3(kkb), -1.0, E_(EX, nxt if d == 1 else 0), ALU.mult, ALU.mult))
                steps(tt(AR[:, :, 1, :], g3(rblk), E_(EX, own if d == 0 else 0), ALU.mult))
                steps(ts(T1[:, :], AA[:, :], col("ka", blk), KAM[:, blk:blk + 1], ALU.mult, ALU.add))
                steps(tt(T2[:, :], kkb, AA[:, :], ALU.mult))
                steps.wait()
                steps(tt(T1[:, :], T1[:, :], kblk, ALU.mult))
                steps(tt(BK[:, 0, :, :], g3(T2[:, :]), E_(EI, own), ALU.mult))
                steps.wait()
                if d == 0:
                    steps(dve.tensor_copy(KS[:, blk, :], T1[:, :]))
                else:
                    steps(tt(KS[:, blk, :], KS[:, blk, :], T1[:, :], ALU.add))
                end, start = (T, 0) if d == 0 else (0, T)
                steps(tt(BK[:, 1, :, :], g3(T1[:, :]), E_(EI, own), ALU.mult))
                steps(ts(S0S[:, :], S0T[:, d * 4 + blk, :], EI[:, 1, start:start + 1], None, ALU.mult))
                steps.wait()
                ts(BKE[:, :, :], BK[:, :, 0, :], EX[:, 0, end:end + 1], None, ALU.mult).then_inc(ev("factors"), 1)
                dve.wait_ge(ev("factors"), i + 1)
                dve.wait_ge(ev("grams"), i + 1)
                for s in range(4):
                    steps(dve.copy_predicated(MAT[:, s, :, :].rearrange("p m t -> p (m t)"),
                                              MASKS[:, d, :, :].rearrange("p m t -> p (m t)"), PS[:, 2 + s, :]))
                for s in range(4):
                    steps(dve.copy_predicated(AS[:, s, :], MASKS[:, 1 - d, 0, :], PS[:, 6 + s // 2, (s % 2) * T:(s % 2 + 1) * T]))
                steps.wait()
                dve.sem_inc(ev("mats"), 1)
                q4 = lambda m: m.rearrange("p (a t) -> p a t", a=1).broadcast_to([P, 4, T])
                ident = q4(IDENT[:, :])
                steps(tt(GM[:, :, :], MAT[:, :, 0, :], q4(LEVEL[:, d, 0, :]), ALU.mult))
                steps(tt(DM[:, :, :], AS[:, :, :], q4(LEVEL[:, 1 - d, 0, :]), ALU.mult))
                steps.wait()
                steps(tt(GM[:, :, :], GM[:, :, :], ident, ALU.add))
                tt(DM[:, :, :], DM[:, :, :], ident, ALU.add).then_inc(ev("inverse"), 1)
                for lv in range(1, LEVELS):
                    n = i * (LEVELS - 1) + lv
                    dve.wait_ge(ev("cross"), n)
                    tt(XS[:, :, :], PS[:, 4, :].rearrange("p (a t) -> p a t", a=4), q4(LEVEL[:, d, lv, :]), ALU.mult)\
                        .then_inc(ev("cross_masked"), 1)
                    dve.wait_ge(ev("update"), n)
                    steps(tt(GM[:, :, :], GM[:, :, :], PS[:, 5, :].rearrange("p (a t) -> p a t", a=4), ALU.add))
                    tt(DM[:, :, :], DM[:, :, :], PS[:, 6, :].rearrange("p (a t) -> p a t", a=4), ALU.add)\
                        .then_inc(ev("inverse"), 1)
                lo, hi = (slice(0, 64), slice(64, 128)) if d == 0 else (slice(64, 128), slice(0, 64))
                rhs = lambda r: PS[r, 2:4, 0:2 * HD]
                four = lambda t_, r: t_[r, :, :].rearrange("p (a b) n -> p a (b n)", a=2)
                dve.wait_ge(ev("rhs"), i + 1)
                dve.tensor_copy(four(RS, lo), rhs(lo)).then_inc(ev("rhs_lo"), 1)
                dve.wait_ge(ev("sa_lo_ps"), i + 1)
                dve.tensor_copy(UU[lo, :, :], PS[lo, 4, 0:4 * HD].rearrange("p (a n) -> p a n", a=4)).then_inc(ev("sa_lo"), 1)
                dve.wait_ge(ev("rhs_hi_ps"), i + 1)
                dve.tensor_copy(four(RS, hi), rhs(hi)).then_inc(ev("rhs_hi"), 1)
                dve.wait_ge(ev("sa_hi_ps"), i + 1)
                dve.tensor_copy(UU[hi, :, :], PS[hi, 5, 0:4 * HD].rearrange("p (a n) -> p a n", a=4)).then_inc(ev("sa_hi"), 1)
                dve.wait_ge(ev("y_ps"), i + 1)
                for hh in range(2):
                    r = slice(HD * hh, HD * hh + HD)
                    src = PS[r, 6 + hh, 0:TOK]
                    if d == 0:
                        last = dve.tensor_copy(YT[r, blk, :], src)
                    else:
                        last = tt(YT[r, blk, :], YT[r, blk, :], src, ALU.add)
                    if hh == 0:
                        steps(last)
                    else:
                        last.then_inc(ev("y_added"), 1)
                dve.wait_ge(ev("y_added"), i + 1)

            def gn(l):
                two = lambda x: x.rearrange("p (a b) t -> p a (b t)", a=2)
                dve.wait_ge(ev("gn_mean"), l + 1)
                tt(two(YT[:, :, :]), two(YT[:, :, :]), PS[:, 2:4, :], ALU.subtract).then_inc(ev("gn_cent"), 1)
                steps(tt(TMP3[:, :, :], RW[:, 0:4, :], KS[:, :, :], ALU.mult))
                steps.wait()
                for b in range(4):
                    last = ts(TMP3[:, b, :], TMP3[:, b, :], col("rk", b), 0.5, ALU.mult, ALU.mult)
                    if b < 3:
                        steps(last)
                last.then_inc(ev("rk_prod"), 1)
                dve.wait_ge(ev("gn_var"), l + 1)
                ts(two(TMP2[:, :, :]), PS[:, 4:6, :], GN_EPS, None, ALU.add).then_inc(ev("gn_eps"), 1)
                dve.wait_ge(ev("gn_root"), l + 1)
                steps(dve.reciprocal(TMP2[:, :, :], TMP2[:, :, :]))
                steps.wait()
                steps(tt(YT[:, :, :], YT[:, :, :], TMP2[:, :, :], ALU.mult))
                dve.wait_ge(ev("bonus"), l + 1)
                steps(tt(two(TMP[:, :, :]), PS[:, 2:4, :], two(RW[:, 8:12, :]), ALU.mult))
                steps.wait()
                for b in range(4):
                    steps(ts(YT[:, b, :], YT[:, b, :], col("gw", b), col("gb", b), ALU.mult, ALU.add))
                steps.wait()
                steps(tt(YT[:, :, :], YT[:, :, :], TMP[:, :, :], ALU.add))
                steps.wait()
                dve.wait_ge(ev("g_ps"), l + 1)
                tt(two(YT[:, :, :]), two(YT[:, :, :]), PS[:, 6:8, :], ALU.mult).then_inc(ev("ya"), 1)
                dve.wait_ge(ev("ya_hi"), l + 1)
                dve.wait_ge(state_out, 16 * 8 * (l + 1))
                steps(tt(YAL[:, :, :], YT[:, :, :], YAH[:, :, :].bitcast(F32), ALU.subtract))

            def sine_argument(bank, c, mark):
                big, two_pi = 12582912.0, 2 * math.pi
                hi_part = 6.28125
                x, k_ = HDT[:, 0, :], HDT[:, 1, :]
                steps(ts(x, PS[0:HID, bank, 0:T], FB[:, c:c + 1], None, ALU.add))
                steps.wait()
                steps(ts(k_, x, 1 / two_pi, big, ALU.mult, ALU.add))
                steps.wait()
                steps(ts(k_, k_, -big, None, ALU.add))
                steps.wait()
                steps(stt(x, k_, -hi_part, x, ALU.mult, ALU.add))
                steps.wait()
                steps(stt(x, k_, -(two_pi - hi_part), x, ALU.mult, ALU.add))
                steps.wait()
                ts(x, x, math.pi - 2e-7, -(math.pi - 2e-7), ALU.min, ALU.max).then_inc(mark, 1)

            def filt(l):
                dve.wait_ge(ev("hid1_ps"), l + 1)
                sine_argument(2, 0, ev("arg1"))
                dve.wait_ge(ev("hid2_ps"), l + 1)
                sine_argument(3, 1, ev("arg2"))
                dve.wait_ge(ev("filt_ps"), l + 1)
                for o in range(4):
                    steps(tt(HS[:, o, :], PS[:, 4 + o, :], WINDOW[:, o % 2, :], ALU.mult))
                steps.wait()
                for o in range(2):
                    f, b = HS[:, 2 * o, :], HS[:, 2 * o + 1, :]
                    steps(tt(f, f, b, ALU.add))
                    steps.wait()
                    last = stt(b, b, 2.0, f, ALU.mult, ALU.subtract)
                    if o == 0:
                        steps(last)
                last.then_inc(ev("filt"), 1)

            def conv(l, o):
                i = l * 2 + o
                kr, krb, ki = KF[:, o, 0, :], KF[:, o, 1, :], KF[:, o, 2, :]
                for g in range(G):
                    dve.wait_ge(ev("zF"), i * 2 + g + 1)
                    zr, zi = PS[:, 4 + 2 * g, :], PS[:, 5 + 2 * g, :]
                    steps(tt(PAB[:, g, 0, :], zr, kr, ALU.mult))
                    steps(tt(CT1[:, :], zi, ki, ALU.mult))
                    steps(tt(PAB[:, g, 1, :], zr, ki, ALU.mult))
                    steps(tt(CT2[:, :], zi, krb, ALU.mult))
                    steps.wait()
                    steps(tt(PAB[:, g, 0, :], PAB[:, g, 0, :], CT1[:, :], ALU.subtract))
                    last = tt(PAB[:, g, 1, :], PAB[:, g, 1, :], CT2[:, :], ALU.add)
                    if g == 0:
                        steps(last)
                        steps.wait()
                last.then_inc(ev("spectrum"), 1)
                dve.wait_ge(ev("conv_ps"), i + 1)
                for b in range(4):
                    steps(stt(HY[:, b, :], HY[:, b, :], col("sk", o * 4 + b), PS[:, 2 + b // 2, (b % 2) * TOK:(b % 2 + 1) * TOK],
                              ALU.mult, ALU.add))
                steps.wait()
                last = tt(HY[:, 0:4, :], HY[:, 0:4, :], HY[:, 4 + 4 * o:8 + 4 * o, :], ALU.mult)
                if o == 0:
                    steps(last)
                else:
                    last.then_inc(ev("yb"), 1)
                    dve.wait_ge(ev("yb_hi"), l + 1)
                    steps(tt(YBL[:, :, :], HY[:, 0:4, :], YBH[:, :, :].bitcast(F32), ALU.subtract))

            def merge(l, i):
                make_lo(number["pb", l, i, 0])
                make_lo(number["pb", l, i, 0] + 1)
                dve.wait_ge(tile_done, number["pb", l, i, 0] + 1)
                two = lambda x: x.rearrange("p b t -> p (b t)")
                for x in range(2):
                    b = 4 * i + 2 * x
                    steps(tt(two(MG[:, b:b + 2, :]), PS[:, 4 * i + x, :], two(SG[:, b:b + 2, :]), ALU.mult))
                    steps(tt(two(MGT[:, :, :]), PS[:, 4 * i + 2 + x, :], two(SG[:, 8 + b:10 + b, :]), ALU.mult))
                    steps.wait()
                    tt(MG[:, b:b + 2, :], MG[:, b:b + 2, :], MGT[:, :, :], ALU.add).then_inc(ev("merged"), 2)
                    dve.wait_ge(ev("merged"), 4 * (l * 2 + i) + 2 * x + 2)
                dve.wait_ge(ev("mg_hi"), l * 2 + i + 1)
                q = slice(4 * i, 4 * i + 4)
                steps(tt(MGL[:, q, :], MG[:, q, :], MGH[:, q, :].bitcast(F32), ALU.subtract))

            def norm(l, w):
                i = l * 2 + w
                if w == 0:
                    for j in range(4):
                        make_lo(number["o", l, j, 0] + 1)
                    last_tile = number["o", l, 3, 0]
                else:
                    last_tile = number["down", l, 10, 0] if l % 2 == 0 else number["down", l, 5, NE - 1]
                dve.wait_ge(tile_done, last_tile + 1)
                dve.wait_ge(ev("gate_rows"), i + 1)
                for g in range(G):
                    gb = GBC[:, g, :].rearrange("p (c n) -> p c n", c=2)
                    xg = X[:, g, :]
                    steps(tt(gb, PS[:, 4 + 2 * g:6 + 2 * g, :], gb, ALU.mult))
                    steps.wait()
                    steps(stt(xg, xg, ALPHA, GBC[:, g, :], ALU.mult, ALU.add))
                    steps.wait()
                    for c in range(2):
                        steps(dve.bn_stats(STAT[:, g, 6 * c:6 * c + 6], xg[:, c * 512:(c + 1) * 512]))
                    steps.wait()
                    steps(dve.bn_aggr(MV[:, g, 0:2], STAT[:, g, :]))
                    steps.wait()
                    ts(MV[:, g, 1:2], MV[:, g, 1:2], LN_EPS, None, ALU.add).then_inc(ev("var"), 1)
                dve.wait_ge(lngb_in, 32 * (i + 1))
                for g in range(G):
                    xg = X[:, g, :]
                    dve.wait_ge(ev("std"), i * 2 + g + 1)
                    steps(dve.reciprocal(MV[:, g, 3:4], MV[:, g, 2:3]))
                    steps.wait()
                    steps(ts(xg, xg, MV[:, g, 0:1], MV[:, g, 3:4], ALU.subtract, ALU.mult))
                    steps.wait()
                    steps(tt(xg, xg, LNGB[:, 0, :], ALU.mult))
                    steps.wait()
                    steps(tt(xg, xg, LNGB[:, 1, :], ALU.add))

            def router(l):
                e3 = lambda x: x.broadcast_to([P, G, NE])
                dve.wait_ge(ev("logits"), 1)
                lg = PS[:, 2, 0:G * NE].rearrange("p (g e) -> p g e", g=G)
                steps(dve.tensor_reduce(SM[:, :, 0:1], lg, AX.X, ALU.max))
                steps.wait()
                tt(LG[:, :, :], lg, e3(SM[:, :, 0:1]), ALU.subtract).then_inc(ev("shifted"), 1)
                dve.wait_ge(ev("exps"), 1)
                steps(dve.tensor_reduce(SM[:, :, 1:2], PR[:, :, :], AX.X, ALU.add))
                steps.wait()
                steps(dve.reciprocal(SM[:, :, 1:2], SM[:, :, 1:2]))
                steps.wait()
                steps(tt(PR[:, :, :], PR[:, :, :], e3(SM[:, :, 1:2]), ALU.mult))
                steps.wait()
                steps(dve.tensor_copy(PW[:, :, :], PR[:, :, :]))
                steps.wait()
                rank = RANK[:, :].rearrange("p (a e) -> p a e", a=1).broadcast_to([P, G, NE])
                for k_ in range(2):
                    steps(dve.tensor_reduce(SM[:, :, 2:3], PW[:, :, :], AX.X, ALU.max))
                    steps.wait()
                    steps(tt(OH[:, :, :], PW[:, :, :], e3(SM[:, :, 2:3]), ALU.is_equal))
                    steps.wait()
                    steps(tt(OH[:, :, :], OH[:, :, :], rank, ALU.mult))
                    steps.wait()
                    steps(dve.tensor_reduce(SM[:, :, 3:4], OH[:, :, :], AX.X, ALU.max))
                    steps.wait()
                    steps(tt(OH[:, :, :], OH[:, :, :], e3(SM[:, :, 3:4]), ALU.is_equal))
                    steps.wait()
                    if k_ == 0:
                        steps(dve.tensor_copy(CMB[:, :, :], OH[:, :, :]))
                    else:
                        steps(tt(CMB[:, :, :], CMB[:, :, :], OH[:, :, :], ALU.add))
                    steps(stt(PW[:, :, :], OH[:, :, :], -2.0, PW[:, :, :], ALU.mult, ALU.add))
                    steps.wait()
                steps(tt(CMB[:, :, :], CMB[:, :, :], PR[:, :, :], ALU.mult))
                steps.wait()
                steps(dve.tensor_reduce(SM[:, :, 2:3], CMB[:, :, :], AX.X, ALU.add))
                steps.wait()
                steps(dve.reciprocal(SM[:, :, 2:3], SM[:, :, 2:3]))
                steps.wait()
                tt(CMB[:, :, :], CMB[:, :, :], e3(SM[:, :, 2:3]), ALU.mult).then_inc(ev("combine"), 1)
                dve.wait_ge(ev("combine"), 1)

            def pair(l, i, e):
                n = number["gate", l, i, e]
                make_lo(n + 1)
                u = pair_no[l, i, e]
                k, w = tile_width(n)
                nb = w // P
                dve.wait_ge(act_read, read_no[n])
                if l % 2 == 1:
                    cb = CB[:, e:e + 1, :].broadcast_to([P, nb, TOK])
                    steps(tt(SL[:, u % 2, 0:nb, :], SL[:, u % 2, 0:nb, :], cb, ALU.mult))
                    steps.wait()
                dve.wait_ge(tile_done, n + 2)
                tt(SL[:, u % 2, 0:nb, :], SL[:, u % 2, 0:nb, :],
                   PS[:, bank_of[n + 1], 0:w * 2].rearrange("p (b t) -> p b t", t=TOK), ALU.mult).then_inc(ev("hidden"), 1)
                dve.wait_ge(ev("hidden"), u + 1)
                dve.sem_inc(dve_read, 1)
                make_lo(n + 2)
                dve.wait_ge(ev("pair_hi"), u + 1)
                o = (0 if l % 2 == 0 else 11 * (e % 2)) + 2 * i
                tt(AL[:, o:o + nb, :], SL[:, u % 2, 0:nb, :], AH[:, o:o + nb, :].bitcast(F32), ALU.subtract)\
                    .then_inc(ev("pair_lo"), 1)
                if (l % 2 == 0 and i == 10) or (l % 2 == 1 and i == 5):
                    steps.wait_for(ev("pair_lo"), u + 1)
                    dve.wait_ge(ev("pair_lo"), u + 1)
                    dve.sem_inc(ev("hidden_lo"), 1)

            def down(l, e):
                for i in range(11 if l % 2 == 0 else 6):
                    make_lo(number["down", l, i, e] + 1)

            k_bar = 0
            for item in sched:
                what, a = item[0], item[1:]
                if what == "barrier":
                    k_bar += 1
                    steps.wait()
                    dve.sem_inc(dve_stage, 1)
                    dve.wait_ge(act_stage, k_bar)
                elif what == "in":
                    mixed(*a)
                elif what == "o":
                    pass
                else:
                    {"cond": cond, "params": params, "ada": ada, "mod": mod, "ht": ht, "wprep": wprep, "batch": batch,
                     "gn": gn, "filter": filt, "conv": conv, "merge": merge, "norm": norm, "router": router,
                     "pair": pair, "down": down}[what](*a)


def kernel(**inputs):
    import concourse.bacc as bacc
    from concourse.bass_utils import run_bass_kernel_spmd

    nc = bacc.Bacc("TRN2", target_bir_lowering=False, num_devices=1)
    arrays, aps = {}, {}
    for name, value in [*inputs.items(), *shape_constants().items()]:
        a = np.ascontiguousarray(value)
        arrays[f"in_{name}"] = a
        aps[name] = nc.dram_tensor(f"in_{name}", a.shape, mybir.dt.from_np(a.dtype), kind="ExternalInput").ap()
    outs = [nc.dram_tensor(f"out_{i}", shape, F32, kind="ExternalOutput").ap()
            for i, shape in enumerate([(1, T, D), (1, T, D), (1, LAYERS, 2, NH, HD, HD)])]
    build(nc, aps, *outs)
    r = run_bass_kernel_spmd(nc, [arrays], core_ids=[0])
    return tuple(r.results[0][f"out_{i}"] for i in range(3))
```

```python
import math
from contextlib import ExitStack

import numpy as np

import concourse.bass as bass
from concourse import mybir

F32 = mybir.dt.float32
F32R = mybir.dt.float32r
U8 = mybir.dt.uint8
ALU = mybir.AluOpType
ACT = mybir.ActivationFunctionType
AX = mybir.AxisListType

P = 128
D = 1024
KB = D // P
T = 128
G = 2
TOK = G * T
LAYERS = 2
DR = 512
NH, HD = 8, 64
RB = 15
HB = 12
GB = 16
D_IN = (RB + HB + GB) * P
DECAY_SCALE = math.exp(-0.5)
GN_EPS = 64e-5
LN_EPS = 1e-5
ALPHA = (2 * LAYERS) ** 0.25
D_FF = 2816
FF_E = 1408
NE = 8
EMB, HID = 33, 64
RING = 3
ADA = 6 * D // 256
TILE = 2048
LEVELS = 7
FIRST_LEVEL, REFINE = 4, 4 + 1 + 2 * (LEVELS - 1)
NREF = 2
OUTPUT = REFINE + 1 + 2 * NREF
STEPS = OUTPUT + 2
FILL_TO = 19

ROWS = [("mu0", RB), ("cw0", HB), ("mu1", RB), ("cw2", HB), ("cw1", HB), ("cb", HB), ("a0", 8), ("kk", 4), ("ka", 4),
        ("rk", 4), ("gw", 4), ("gb", 4), ("sk", 8), ("w0", 8)]
ROW_AT, NROW = {}, 0
for _name, _n in ROWS:
    ROW_AT[_name] = NROW
    NROW += _n


def shape_constants():
    i = np.arange(P)
    s, t = i[:, None], i[None, :]
    j = np.arange(T + 1)[None, :]
    tri = np.stack([(s < j) * 1.0 - (s < T // 2), (s >= j) * 1.0 - (s >= T // 2)], 1)
    ang = 2 * np.pi * (s * t % 256) / 256
    nyq = (-1.0) ** i
    cos_a, sin_a = np.cos(ang), np.sin(ang)
    cos_b, sin_b = cos_a.copy(), -sin_a
    cos_b[:, 0] = nyq
    sin_b = sin_b.copy()
    sin_b[:, 0] = nyq
    inv_c, inv_s = 2 * cos_a / 256, -2 * sin_a / 256
    inv_c[0, :] = 1 / 256
    inv_s[0, :] = nyq / 256
    dft = np.stack([cos_a, cos_b, sin_a, sin_b, inv_c, inv_s], 1)
    masks = np.zeros((P, 2, 4, P))
    for d, (strict, incl) in enumerate((((s < t), (s <= t)), ((s > t), (s >= t)))):
        for m, w in enumerate((strict, incl, strict, incl)):
            masks[:, d, m] = w
    level = np.zeros((P, 2, LEVELS, P))
    for lv in range(LEVELS):
        h = 1 << lv
        same = s // (2 * h) == t // (2 * h)
        level[:, 0, lv] = same & ((s // h) % 2 == 0) & ((t // h) % 2 == 1)
        level[:, 1, lv] = same & ((s // h) % 2 == 1) & ((t // h) % 2 == 0)
    lin = np.linspace(0.0, 1.0, T, dtype=np.float32)
    f = np.linspace(1e-4, 15, 16, dtype=np.float32)
    a = np.float32(2 * math.pi / T) * np.arange(T, dtype=np.float32)[:, None] * f
    feats = np.concatenate([lin[:, None], np.cos(a), -np.sin(a)], 1)
    deltas = np.abs(np.linspace(math.log(1e-2) / 1.5, math.log(1e-2) / 0.3, DR, dtype=np.float32))
    window = np.exp(-lin[:, None] * deltas)
    window_b = window.copy()
    window_b[0] = 0
    omega = 1.0 / (10000.0 ** (np.arange(256, dtype=np.float32) / 256))
    enc = lambda pos: np.concatenate([np.sin(pos[:, None] * omega), np.cos(pos[:, None] * omega)], -1)
    pos = np.concatenate([enc((i // 64).astype(np.float32)), enc((i % 64).astype(np.float32))], -1)
    head = (s // HD == t // HD) * 1.0
    f4 = lambda x: np.ascontiguousarray(x, dtype=np.float32)
    return {"c_ident": f4(np.eye(P)), "c_tri": f4(tri), "c_dft": f4(dft), "c_masks": f4(masks), "c_level": f4(level),
            "c_feats": f4(feats.T), "c_window": f4(np.stack([window, window_b], 1)), "c_pos": f4(pos),
            "c_head": f4(np.stack([head, head / HD], 1)), 
            "c_rank": f4(np.broadcast_to(NE - np.arange(NE), (P, NE)))}


def schedule():
    sched = [("cond",)]
    for j in range(ADA):
        sched.append(("ada", 0, j, 0, 2))
        sched += [("turn", 0, j - 1), ("col", 0, j - 1)] if j else [("bias",)]
        sched += [("ada", 0, j, 1, 2), ("row", 0, j)]
    sched += [("turn", 0, ADA - 1), ("col", 0, ADA - 1), ("consts",), ("params", 0), ("barrier",)]

    def norm(l, w, turned):
        items = [("gates", l, w), ("resid", l, w, 0), ("z", l, w, 0), ("resid", l, w, 1), ("z", l, w, 1)]
        if turned:
            items += [("ht", *turned, 0), ("ht", *turned, 1), ("ht_done", *turned)]
        return items + [("affine", l, w)]

    sched += [("ht", 0, 0, 0), ("ht", 0, 0, 1), ("ht_done", 0, 0)]
    for l in range(LAYERS):
        sched += [("in", l, i) for i in range(5)] + [("keys", l), ("in", l, 5), ("key_norms", l), ("in", l, 6)]
        sched += [("values", l), ("in", l, 7), ("wprep", l), ("barrier",)]
        fill, pieces = [], 8 if l + 1 < LAYERS else 4
        for i in range(8, FILL_TO):
            fill += [(("part", l, i, p, pieces), []) for p in range(pieces)]
            fill[-1] = (fill[-1][0], [(1, ("later", l, i))])
            for j in range(ADA * (i - 8) // (FILL_TO - 8), ADA * (i - 7) // (FILL_TO - 8) if l + 1 < LAYERS else 0):
                fill += [(("ada", l + 1, j, p, 4), []) for p in range(4)]
                fill[-1] = (fill[-1][0], [(1, ("row", l + 1, j)), (2, ("turn", l + 1, j)), (3, ("col", l + 1, j))])
        slots, slot, used, pending = 8 * STEPS, 0, 0, []
        for clock in range(STEPS // 2 * 7 + STEPS):
            for b in range(8):
                if not 0 <= clock - b * (STEPS // 2) < STEPS:
                    continue
                sched.append(("scan", l, b, clock - b * (STEPS // 2)))
                slot += 1
                if slot * len(fill) // slots > used:
                    sched += [item for due, item in pending if due == used]
                    pending = [(due, item) for due, item in pending if due > used]
                    piece, later = fill[used]
                    sched.append(piece)
                    pending += [(used + delay, item) for delay, item in later]
                    used += 1
        sched += [item for due, item in sorted(pending)]
        rest = [[("part", l, i, 0, 1), ("later", l, i)] for i in range(FILL_TO, 22)]
        sched += [("barrier",), ("gn", l, 0), rest[0][0], ("gn", l, 1), rest[0][1], rest[1][0], ("gn", l, 2), rest[1][1],
                  rest[2][0], ("sines", l), rest[2][1]]
        sched += [("barrier",), ("filter", l), ("conv", l, 0), ("conv", l, 1)]
        sched += [("merge", l, 0), ("merge", l, 1), ("o", l)] + norm(l, 0, (l, 1))
        sched += [("params", l + 1)] if l + 1 < LAYERS else []
        if l % 2 == 0:
            sched += [("pair", l, i, 0) for i in range(11)] + [("down", l, 0)]
        else:
            sched += [("router", l)]
            for e in range(NE):
                sched += [("pair", l, i, e) for i in range(6)] + [("down", l, e)]
        sched += norm(l, 1, (l + 1, 0) if l + 1 < LAYERS else None)
    sched.append(("barrier",))
    tiles = []
    for what, *a in sched:
        if what == "in" or what in ("ada", "part") and a[2] == 0:
            tiles.append(("ada" if what == "ada" else "in", a[0], a[1], 0))
        elif what == "merge":
            tiles += [("pa", a[0], a[1], 0), ("pb", a[0], a[1], 0)]
        elif what == "o":
            tiles += [("o", a[0], i, 0) for i in range(4)]
        elif what == "pair":
            tiles += [("gate", *a), ("up", *a)]
        elif what == "down":
            tiles += [("down", a[0], i, a[1]) for i in range(11 if a[0] % 2 == 0 else 6)]
    return sched, tiles


def in_blocks(i):
    if i < 7:
        return [2 * i, 2 * i + 1]
    if i == 7:
        return [14]
    return [RB + 2 * (i - 8), RB + 2 * (i - 8) + 1]


class Steps:

    def __init__(self, engine, own):
        self.engine, self.own, self.count, self.also = engine, own, 0, []

    def __call__(self, instruction):
        self.count += 1
        instruction.then_inc(self.own, 1)

    def wait_for(self, other, value):
        self.also.append((other, value))

    def wait(self):
        if self.count:
            self.engine.wait_ge(self.own, self.count)
        for other, value in self.also:
            self.engine.wait_ge(other, value)
        self.also = []


def build(nc, A, y_prompt, y_sample, new_state):
    ctx = ExitStack()
    with ctx:
        cursor = [16512]

        def sb(name, shape, dt=F32, at=None):
            size = int(np.prod(shape[1:])) * (1 if dt == U8 else 4)
            size = (size + 31) // 32 * 32
            if at is None:
                at = cursor[0]
                cursor[0] += size
            return nc.alloc_sbuf_tensor_at(name, shape, dt, offset=at)

        def sem(name):
            return ctx.enter_context(nc.semaphore(name))

        X = sb("X", [P, G, D])
        hth_at = cursor[0]
        HTH = sb("HTH", [P, KB, TOK], F32R)
        HTL = sb("HTL", [P, KB, TOK], F32R)
        MGH = sb("MGH", [P, KB, TOK], F32R, at=hth_at)
        MGL = sb("MGL", [P, KB, TOK], F32R, at=hth_at + KB * TOK * 4)
        IDENT = sb("IDENT", [P, P])
        TRI = sb("TRI", [P, 2, T + 1])
        DFT = sb("DFT", [P, 6, P])
        MASKS = sb("MASKS", [P, 2, 4, P], U8)
        LEVEL = sb("LEVEL", [P, 2, LEVELS, P], U8)
        HEAD = sb("HEAD", [P, 2, P])
        FEATS = sb("FEATS", [EMB, T])
        ONES = sb("ONES", [1, P])
        IDR = sb("IDR", [P, P], F32R)
        RANK = sb("RANK", [P, NE])
        PROW = sb("PROW", [NROW, P])
        BROW = sb("BROW", [48, LAYERS, P])
        PT = sb("PT", [P, NROW])
        CEN = sb("CEN", [P, RB])
        KAM = sb("KAM", [P, 4])
        KAH = sb("KAH", [P, 4])
        A0H = sb("A0H", [P, 8])
        BADT = sb("BADT", [P, LAYERS, 48])
        LNT = sb("LNT", [P, LAYERS, 4 * KB])
        FOLD = sb("FOLD", [P, KB, 2])
        MODT = sb("MODT", [P, LAYERS, 48, 2])
        COND = sb("COND", [16, P])
        CONDT = sb("CONDT", [P, 16])
        ADAR = sb("ADAR", [2, 2, 256])
        A2 = sb("A2", [P, DR])
        G2 = sb("G2", [P, DR])
        F1 = sb("F1", [EMB, HID])
        F2 = sb("F2", [HID, HID])
        FB = sb("FB", [HID, 2])
        RW_ = sb("RW_", [P, KB, NE])
        RWH = sb("RWH", [P, KB, NE], F32R)
        RWL = sb("RWL", [P, KB, NE], F32R)
        RBIAS = sb("RBIAS", [1, NE])
        STAT = sb("STAT", [P, 2, 12])
        MV = sb("MV", [P, 2, 4])
        WRING = sb("WRING", [P, RING, TILE])
        WH = sb("WH", [P, 2, TILE], F32R)
        WL = sb("WL", [P, 2, TILE], F32R)
        base = cursor[0]
        room = 229344 - base

        def at(start, name, shape, dt=F32):
            size = int(np.prod(shape[1:])) * 4
            assert start * 4 + size <= room, (name, start * 4 + size, room)
            return sb(name, shape, dt, at=base + start * 4)

        RW = at(0, "RW", [P, RB, TOK])
        SGW = at(3840, "SGW", [P, 4, DR])
        VT = at(5888, "VT", [P, G, DR])
        KK = at(6912, "KK", [P, 4, TOK])
        YT = at(6912, "YT", [P, 4, TOK])
        KSF = at(7936, "KSF", [P, TOK])
        S0T = at(8192, "S0T", [P, 8, HD])
        S0R = at(8704, "S0R", [HD, 2, NH, HD])
        HY = at(8704, "HY", [P, HB, TOK])
        SG = at(11776, "SG", [P, GB, TOK])
        W2 = at(24064, "W2", [P, DR])
        WLOW = RW[:, 12, :]
        GLOW = RW[:, 14, :]
        KS = RW[:, 4:8, :]
        LANE, LANES = 6400, 11776 + 2 * (FILL_TO - 14) * TOK

        def lane(start, name, shape, dt=F32):
            return [at(LANES + k_ * LANE + start, f"{name}{k_}", shape, dt) for k_ in range(2)]

        AR = lane(0, "AR", [P, G, 2, T])
        BK = lane(512, "BK", [P, 2, G, T])
        BKT = lane(512, "BKT", [P, 2, T])
        BKW = lane(512, "BKW", [P, 4, HD])
        RR = lane(768, "RR", [P, 4, HD], F32R)
        MAT = lane(1024, "MAT", [P, 4, 4, T])
        AS = lane(3072, "AS", [P, 4, T], F32R)
        GM = lane(3584, "GM", [P, 4, T], F32R)
        DM = lane(4096, "DM", [P, 4, T], F32R)
        XS = lane(4608, "XS", [P, 4, T], F32R)
        EX = lane(3072, "EX", [P, G, T + 1])
        EI = lane(3336, "EI", [P, G, T + 1])
        AA = lane(3600, "AA", [P, TOK])
        T1 = lane(4608, "T1", [P, TOK])
        T2 = lane(4864, "T2", [P, TOK])
        RS = lane(5120, "RS", [P, 4, HD])
        SFS = lane(5120, "SFS", [HD, 2, HD])
        RSR = lane(5376, "RSR", [P, 4, HD], F32R)
        UU = lane(5632, "UU", [P, 4, HD])
        BKE = lane(5888, "BKE", [P, 2, T])
        S0P = lane(6144, "S0P", [P, 2, HD])
        TMP = at(15872, "TMP", [P, 4, TOK])
        TMP2 = at(16896, "TMP2", [P, 4, TOK])
        TMP3 = at(17920, "TMP3", [P, 4, TOK])
        YAH = at(22016, "YAH", [P, 4, TOK], F32R)
        YAL = at(23040, "YAL", [P, 4, TOK], F32R)
        F3 = at(25088, "F3", [HID, 4, DR])
        HS = at(2048, "HS", [P, 4, DR])
        CT1 = at(2048, "CT1", [P, G, DR])
        CT2 = at(3072, "CT2", [P, G, DR])
        WINDOW = at(4096, "WINDOW", [P, 2, DR])
        YBH = at(5120, "YBH", [P, 4, TOK], F32R)
        YBL = at(6144, "YBL", [P, 4, TOK], F32R)
        HD1 = at(24576, "HD1", [HID, 2, T])
        HDT = at(24832, "HDT", [HID, 2, T])
        MGT = at(7680, "MGT", [P, 2, TOK])
        MG = at(0, "MG", [P, KB, TOK])
        KF = at(15872, "KF", [P, 2, 3, DR])
        ZT = at(18944, "ZT", [P, G, DR])
        PAB = at(19968, "PAB", [P, G, 2, DR])
        AH = at(0, "AH", [P, 22, TOK], F32R)
        AL = at(5632, "AL", [P, 22, TOK], F32R)
        CB = at(11264, "CB", [P, NE, TOK])
        GBC = at(13312, "GBC", [P, G, D])
        LNGB = at(15360, "LNGB", [P, 2, D])
        SL = at(17408, "SL", [P, 2, 2, TOK])
        HTF = at(18432, "HTF", [P, KB, TOK])
        POS = at(13312, "POS", [P, D])
        MASKF = at(0, "MASKF", [P, 2, 4, P])
        LNR = at(3072, "LNR", [4 * KB, LAYERS, P])
        LEVELF = at(1024, "LEVELF", [P, 2, LEVELS, P])
        LG = at(10240, "LG", [P, G, NE])
        PR = at(10256, "PR", [P, G, NE])
        OH = at(10272, "OH", [P, G, NE])
        PW = at(10288, "PW", [P, G, NE])
        CMB = at(10304, "CMB", [P, G, NE])
        SM = at(10320, "SM", [P, G, 4])
        CTT = at(10336, "CTT", [NE, TOK])

        PS = ctx.enter_context(nc.psum_tensor("PS", [P, 8, 512], F32))

        sched, tiles = schedule()
        NT = len(tiles)
        number = {t: n for n, t in enumerate(tiles)}
        split_no, k = [], 0
        for t in tiles:
            split_no.append(k)
            k += t[0] != "ada"
        ring_in = [sem(f"ring_in{i}") for i in range(RING)]
        tile_done = sem("tile_done")
        hi_ready = sem("hi_ready")
        lo_ready = sem("lo_ready")

        def split(n):
            return tiles[n][0] != "ada"

        def tile_width(n):
            kind, l, i, e = tiles[n]
            if kind == "in" and i == 7:
                return (KB, P)
            if kind == "ada" or kind == "in":
                return (KB, 256)
            if kind in ("gate", "up"):
                return (KB, 256 if l % 2 == 0 or i < 5 else P)
            if kind in ("pa", "pb"):
                return (4, 512)
            if kind == "down" and l % 2 == 1 and i == 5:
                return (1, D)
            return (2, D)

        def tile_view(tensor, slot, n):
            k, w = tile_width(n)
            return tensor[:, slot, 0:k * w].rearrange("p (k w) -> p k w", k=k)

        def tile_source(n):
            kind, l, i, e = tiles[n]
            k, w = tile_width(n)
            if kind == "ada":
                src = A["w_ada"][l, :, i * 256:(i + 1) * 256]
            elif kind == "in":
                b = in_blocks(i)[0]
                src = A["w_in"][l, :, b * P:b * P + w]
            elif kind in ("pa", "pb"):
                src = A["w_" + kind][l, :, i * 512:(i + 1) * 512]
            elif kind == "o":
                src = A["w_o"][l, i * 256:(i + 1) * 256, :]
            elif kind in ("gate", "up"):
                half = D_FF if l % 2 == 0 else FF_E
                c = (kind == "up") * half + i * 256
                src = (A["ffn_w_in"][l // 2] if l % 2 == 0 else A["exp_w_in"][l // 2, e])[:, c:c + w]
            else:
                src = (A["ffn_w_out"][l // 2] if l % 2 == 0 else A["exp_w_out"][l // 2, e])[i * 256:i * 256 + k * P, :]
            return src.rearrange("(k p) w -> p k w", p=P)

        reader = []
        for kind, l, i, e in tiles:
            reader.append({"ada": "dve", "in": "act" if i >= 14 else "dve", "gate": "act", "up": "dve"}.get(kind))
        read_no = [sum(r == reader[n] for r in reader[:n + 1]) for n in range(NT)]
        bank_of, last_in_bank = [None] * NT, [None] * NT
        u, held = 0, {}
        for n, (kind, l, i, e) in enumerate(tiles):
            if reader[n]:
                bank_of[n] = u % 2
                last_in_bank[n] = held.get(u % 2)
                held[u % 2] = n
                u += 1
        pairs = [t[1:] for t in tiles if t[0] == "gate"]
        pair_no = {t: u for u, t in enumerate(pairs)}

        def act_reads_through(l):
            return read_no[max(n for n, t in enumerate(tiles) if t[0] == "gate" and t[1] == l)]

        def dve_reads_through(l):
            return read_no[max(n for n, t in enumerate(tiles) if t[0] == "up" and t[1] == l)]

        def behind_norm(i):
            l, w = divmod(i, 2)
            return number[("o", l, 3, 0) if w == 0 else ("down", l, 10 if l % 2 == 0 else 5, 0 if l % 2 == 0 else NE - 1)] + 2

        act_read = sem("act_read")
        dve_read = sem("dve_read")

        barriers, seen = {}, 0
        for at_, item in enumerate(sched):
            barriers[at_] = seen
            seen += item[0] == "barrier"
        first_of = {}
        for at_, item in enumerate(sched):
            first_of.setdefault(item, at_)

        def barrier_after(item):
            return barriers[first_of[item]] + 1

        act_stage = sem("act_stage")
        dve_stage = sem("dve_stage")
        E = {}

        def ev(name):
            if name not in E:
                E[name] = sem(name)
            return E[name]

        const_in = sem("const_in")
        cond_in = sem("cond_in")
        bias_in = sem("bias_in")
        x_in = sem("x_in")
        param_in = sem("param_in")
        lngb_in = sem("lngb_in")
        s0_in = sem("s0_in")
        f3_in = sem("f3_in")
        y_out = sem("y_out")
        CONSTS = [(TRI, "c_tri"), (DFT, "c_dft"), (MASKF, "c_masks"), (LEVELF, "c_level"),
                  (HEAD, "c_head"), (FEATS, "c_feats"),
                  (RANK, "c_rank"), (POS, "c_pos")]
        NCONST = 16 * len(CONSTS)
        NCOND = 16 * 3
        NPARAM = 16 * (len(ROWS) + 3 + 4 + 2)

        block = ctx.enter_context(nc.Block())

        @block.sync
        def _(sp):
            for n in range(NT):
                if n >= RING:
                    old = n - RING
                    if split(old):
                        sp.wait_ge(lo_ready, split_no[old] + 1)
                    else:
                        sp.wait_ge(tile_done, old + 1)
                sp.dma_start(tile_view(WRING, n % RING, n), tile_source(n)).then_inc(ring_in[n % RING], 16)
            for g, y in enumerate((y_prompt, y_sample)):
                sp.wait_ge(ev("affine"), 4 * (LAYERS - 1) + 2 + g + 1)
                sp.dma_start(y[0], X[:, g, :]).then_inc(y_out, 16)
            sp.wait_ge(y_out, 32)
            for x in range(2):
                sp.wait_ge(ev(f"state_out{x}"), 16 * LAYERS * 4)

        @block.gpsimd
        def _(pool):
            steps = Steps(pool, sem("pool_steps"))
            pool.memset(ONES[:, :], 1.0).then_inc(ev("ones_set"), 1)
            for dst, name in CONSTS:
                pool.dma_start(dst[:], A[name]).then_inc(const_in, 16)

            def layer_params(l):
                srcs = {"mu0": A["rwkv_mu"][l, 0], "mu1": A["rwkv_mu"][l, 1], "cw0": A["hy_conv_w"][l, 0],
                        "cw1": A["hy_conv_w"][l, 1], "cw2": A["hy_conv_w"][l, 2], "cb": A["hy_conv_b"][l],
                        "a0": A["rwkv_a0"][l].rearrange("d n -> (d n)"), "kk": A["rwkv_k_k"][l],
                        "ka": A["rwkv_k_a"][l], "rk": A["rwkv_r_k"][l].rearrange("h n -> (h n)"),
                        "gw": A["rwkv_gn_w"][l], "gb": A["rwkv_gn_b"][l],
                        "sk": A["hy_skip"][l].rearrange("d n -> (d n)"),
                        "w0": A["rwkv_w0"][l].rearrange("d n -> (d n)")}
                for name, n in ROWS:
                    pool.dma_start(PROW[ROW_AT[name]:ROW_AT[name] + n, :],
                                   srcs[name].rearrange("(b p) -> b p", p=P)).then_inc(param_in, 16)
                pool.dma_start(W2[:, :], A["rwkv_w2"][l].rearrange("d k n -> (d k) n")).then_inc(param_in, 16)
                pool.dma_start(A2[:, :], A["rwkv_a2"][l].rearrange("d k n -> (d k) n")).then_inc(param_in, 16)
                pool.dma_start(G2[:, :], A["rwkv_g2"][l]).then_inc(param_in, 16)
                pool.dma_start(F1[:, :], A["hy_f1"][l]).then_inc(param_in, 16)
                pool.dma_start(F2[:, :], A["hy_f2"][l]).then_inc(param_in, 16)
                pool.dma_start(FB[:, 0:1], A["hy_fb1"][l].rearrange("(p a) -> p a", a=1)).then_inc(param_in, 16)
                pool.dma_start(FB[:, 1:2], A["hy_fb2"][l].rearrange("(p a) -> p a", a=1)).then_inc(param_in, 16)
                pool.dma_start(RW_[:, :, :], A["router_w"][0].rearrange("(k p) e -> p k e", p=P)).then_inc(param_in, 16)
                pool.dma_start(RBIAS[:, :], A["router_b"]).then_inc(param_in, 16)

            def keys_of(l, b):
                blk, d = b // 2, b % 2
                j, x = l * 4 + blk, d
                own = 1 - d
                end = T if d == 0 else 0
                ei, t1 = EI[x], T1[x]
                if blk:
                    pool.wait_ge(ev(f"state_ps{x}"), j)
                pool.wait_ge(ev(f"decays{x}"), j + 1)
                steps(pool.tensor_scalar(t1[:, :], AA[x][:, :], KAH[:, blk:blk + 1], KAM[:, blk:blk + 1], ALU.mult, ALU.add))
                steps.wait()
                steps(pool.tensor_tensor(t1[:, :], t1[:, :], RW[:, 4 + blk, :], ALU.mult))
                steps.wait()
                pool.tensor_tensor(BK[x][:, 1, :, :], t1[:, :].rearrange("p (g t) -> p g t", g=G), ei[:, :, own:own + T],
                                   ALU.mult).then_inc(ev(f"kappa{x}"), 1)
                if d == 0:
                    steps(pool.tensor_copy(KSF[:, :], t1[:, :]))
                else:
                    steps(pool.tensor_tensor(KS[:, blk, :], KSF[:, :], t1[:, :], ALU.add))
                steps.wait()
                pool.wait_ge(ev(f"factors{x}"), j + 1)
                pool.wait_ge(ev(f"kappa{x}"), j + 1)
                pool.tensor_scalar(BKE[x][:, :, :], BK[x][:, :, 0, :], EX[x][:, 0, end:end + 1], None, ALU.mult)\
                    .then_inc(ev(f"ends{x}"), 1)

            def stage_wait(item):
                pool.wait_ge(act_stage, barrier_after(item))
                pool.wait_ge(dve_stage, barrier_after(item))

            for l in range(LAYERS):
                if l == 0:
                    layer_params(l)
                if l > 0:
                    pool.wait_ge(tile_done, max(n for n, t in enumerate(tiles) if t[:2] == ("down", l - 1)) + 1)
                pool.dma_start(S0R[:, :, :, :], A["state_wkv"][0, l].rearrange("d h v k -> v d h k"))\
                    .then_inc(s0_in, 16)
                pool.wait_ge(ev("kk_done"), l + 1)
                for x in range(2):
                    pool.memset(S0P[x][:, :, :], 0.0).then_inc(ev("zeros"), 1)
                for x in range(2):
                    pool.memset(MAT[x][:, :, :, :], 0.0).then_inc(ev("zeros"), 1)
                for b in range(8):
                    keys_of(l, b)
                stage_wait(("scan", l, 7, STEPS - 1))
                for x in range(2):
                    pool.wait_ge(ev(f"state_out{x}"), 16 * 4 * (l + 1))
                pool.dma_start(WINDOW[:, :, :], A["c_window"]).then_inc(f3_in, 16)
                pool.dma_start(F3[:, :, :], A["hy_f3"][l].rearrange("k (o n) -> k o n", n=DR)).then_inc(f3_in, 16)
                for w in range(2):
                    if w == 0:
                        pool.wait_ge(ev("mg_lo"), 2 * l + 2)
                    else:
                        pool.wait_ge(ev("affine"), 4 * l + 2)
                    pool.dma_start(LNGB[:, 0, :], A["ln_g"][l, w:w + 1, :].broadcast_to([P, D])).then_inc(lngb_in, 16)
                    pool.dma_start(LNGB[:, 1, :], A["ln_b"][l, w:w + 1, :].broadcast_to([P, D])).then_inc(lngb_in, 16)
                    if w == 0 and l + 1 < LAYERS:
                        layer_params(l + 1)

        @block.tensor
        def _(pe):
            mm = pe.matmul

            def ready(n):
                if split(n):
                    pe.wait_ge(hi_ready, split_no[n] + 1)
                    pe.wait_ge(lo_ready, split_no[n] + 1)
                else:
                    pe.wait_ge(ring_in[n % RING], 16 * (n // RING + 1))

            def bank_free(n):
                old = last_in_bank[n]
                if old is not None:
                    pe.wait_ge(act_read if reader[old] == "act" else dve_read, read_no[old])

            def product(n, hi, lo, part=0, parts=1):
                if part == 0:
                    ready(n)
                    bank_free(n)
                k, w = tile_width(n)
                h, s = tile_view(WH, split_no[n] % 2, n), tile_view(WL, split_no[n] % 2, n)
                work = [(b, kb) for b in range(w // P) for kb in range(k)]
                for b, kb in work[len(work) * part // parts:len(work) * (part + 1) // parts]:
                    out = PS[:, bank_of[n], b * TOK:(b + 1) * TOK]
                    c = slice(b * P, (b + 1) * P)
                    mm(out, h[:, kb, c], hi[:, kb, :], start=kb == 0, stop=False)
                    mm(out, h[:, kb, c], lo[:, kb, :], start=False, stop=False)
                    last = mm(out, s[:, kb, c], hi[:, kb, :], start=False, stop=kb == k - 1)
                if part == parts - 1:
                    last.then_inc(tile_done, 1)

            def cond():
                pe.wait_ge(cond_in, NCOND)
                pe.transpose(PS[:, 2, 0:16], COND[:, :], IDENT[0:16, 0:16]).then_inc(ev("start_ps"), 1)
                pe.wait_ge(ev("cond_silu"), 1)

            def bias():
                pe.wait_ge(bias_in, 16 * 5)
                for x in range(LAYERS):
                    pe.transpose(PS[:, 4, 64 * x:48 + 64 * x], BROW[:, x, :], IDENT[0:48, 0:48])
                    last = pe.transpose(PS[:, 4, 128 + 32 * x:160 + 32 * x], LNR[:, x, :], IDENT[0:32, 0:32])
                last.then_inc(ev("start_ps"), 1)

            def consts():
                pe.wait_ge(const_in, NCONST)
                pe.wait_ge(ev("ones_set"), 1)

            def params(l):
                pe.wait_ge(param_in, NPARAM * (l + 1))
                pe.transpose(PS[:, 3, 0:NROW], PROW[:, :], IDENT[0:NROW, 0:NROW]).then_inc(ev("paramT"), 1)

            def ada(l, j, part, parts):
                n = number["ada", l, j, 0]
                if part == 0:
                    ready(n)
                    bank_free(n)
                w = tile_view(WRING, n % RING, n)
                for kb in range(KB * part // parts, KB * (part + 1) // parts):
                    last = mm(PS[0:2, bank_of[n], 0:256], CONDT[:, kb::8], w[:, kb, :], start=kb == 0, stop=kb == KB - 1)
                if part == parts - 1:
                    last.then_inc(tile_done, 1)

            def turn(l, j):
                n = number["ada", l, j, 0]
                pe.wait_ge(ev("ada_row"), l * ADA + j + 1)
                for b in range(2):
                    last = pe.transpose(PS[:, bank_of[n], 256 + 2 * b:258 + 2 * b], ADAR[:, j % 2, b * P:(b + 1) * P],
                                        IDENT[0:2, 0:2])
                last.then_inc(ev("ada_turn"), 1)

            def ht(l, w, g):
                if l + w:
                    pe.wait_ge(ev("z"), (2 * l + w - 1) * 2 + g + 1)
                elif g == 0:
                    pe.wait_ge(ev("params_read"), 1)
                for kb in range(KB):
                    last = pe.transpose(PS[:, 2 + 2 * g + kb // 4, (kb % 4) * P:(kb % 4 + 1) * P],
                                        X[:, g, kb * P:(kb + 1) * P], IDENT[:, :])
                    if kb % 4 == 3:
                        last.then_inc(ev("xT"), 1)

            def key_norms(l):
                pe.wait_ge(ev("kk_sq"), l + 1)
                for b in range(4):
                    last = mm(PS[:, 2 + b // 2, (b % 2) * TOK:(b % 2 + 1) * TOK], HEAD[:, 0, :], TMP[:, b, :],
                              start=True, stop=True)
                last.then_inc(ev("kk_norm"), 1)

            def wprep(l):
                pe.wait_ge(ev("wlow"), l + 1)
                pe.wait_ge(ev("kk_max"), l + 1)
                for d in range(2):
                    for g in range(G):
                        q = slice(HD * d, HD * d + HD)
                        mm(PS[:, 2 + 2 * d + g, :], WLOW[q, g * T:(g + 1) * T], W2[q, :], start=True, stop=False, skip_group_check=True)
                        for b in range(4):
                            w0 = ROW_AT["w0"] + d * 4 + b
                            last = mm(PS[:, 2 + 2 * d + g, b * P:(b + 1) * P], PT[:, w0:w0 + 1].broadcast_to([P, P]),
                                      IDENT[:, :], start=False, stop=True, skip_group_check=True)
                        last.then_inc(ev("w_pre"), 1)
                for g in range(G):
                    for b in range(4):
                        last = pe.transpose(PS[:, 6 + g, b * P:(b + 1) * P], RW[:, 8 + b, g * T:(g + 1) * T], IDENT[:, :])
                    last.then_inc(ev("vT"), 1)
                pe.wait_ge(s0_in, 16 * (l + 1))
                pe.wait_ge(ev("sgw"), 4 * l + 3)
                for d in range(2):
                    for b in range(4):
                        o = (d * 4 + b) * HD
                        last = pe.transpose(PS[:, 4, o:o + HD],
                                            S0R[:, d, 2 * b:2 * b + 2, :].rearrange("v h k -> v (h k)"),
                                            IDENT[0:HD, 0:HD])
                last.then_inc(ev("s0T"), 1)

            def scan(l, b, step):
                i, blk, d = l * 8 + b, b // 2, b % 2
                j, x = l * 4 + blk, d
                bk = [2 + 3 * x, 3 + 3 * x, 4 + 3 * x]
                four = lambda bank, s: PS[:, bank, s * T:(s + 1) * T]
                half = lambda bank, s: PS[:, bank, s * HD:(s + 1) * HD]

                def gram(s, bank):
                    r = slice(HD * (s // 2), HD * (s // 2) + HD)
                    ar = AR[x][r, s % 2, :, :].rearrange("p a t -> p (a t)")
                    mm(PS[:, bank, 0:256], BK[x][r, 0, s % 2, :], ar, start=True, stop=True)
                    return mm(PS[:, bank, 256:512], BK[x][r, 1, s % 2, :], ar, start=True, stop=True)

                if step == 0:
                    if blk:
                        pe.wait_ge(ev(f"y_added{x}"), j)
                        pe.wait_ge(ev(f"bk_copied{x}"), j)
                    for g in range(G):
                        mm(PS[:, bk[0], g * 129:(g + 1) * 129], SGW[:, d * 2 + g, blk * P:(blk + 1) * P], TRI[:, d, :],
                           start=True, stop=True)
                    q = slice(HD * d, HD * d + HD)
                    mm(PS[:, bk[1], 0:TOK], A2[q, blk * P:(blk + 1) * P], RW[q, 13, :], start=True, stop=True)\
                        .then_inc(ev(f"decay_sum{x}"), 1)
                elif step == 1:
                    pe.wait_ge(ev(f"factors{x}"), j + 1)
                    pe.wait_ge(ev(f"kappa{x}"), j + 1)
                    if blk:
                        pe.wait_ge(ev(f"state_copied{x}"), j)
                    for s in range(3):
                        last = gram(s, bk[s])
                        last.then_inc(ev(f"gram{x}"), 1)
                elif step == 2:
                    pe.wait_ge(ev(f"masked{x}"), 4 * j + 1)
                    gram(3, bk[0]).then_inc(ev(f"gram{x}"), 1)
                    pe.wait_ge(ev(f"masked{x}"), 4 * j + 3)
                    for s in range(3):
                        pe.transpose(four(bk[1], s), MAT[x][:, s, 0, :], IDENT[:, :])
                elif step == 3:
                    pe.wait_ge(ev(f"masked{x}"), 4 * j + 4)
                    pe.transpose(four(bk[1], 3), MAT[x][:, 3, 0, :], IDENT[:, :]).then_inc(ev(f"turned{x}"), 1)
                    pe.wait_ge(ev(f"ends{x}"), j + 1)
                    for s in (1, 3, 0, 2):
                        v = slice((2 * blk + s // 2) * HD, (2 * blk + s // 2 + 1) * HD)
                        if s % 2:
                            mm(half(bk[2], s), AR[x][:, 1, 0, :], S0P[x][:, s // 2, :], start=s == 1, stop=False,
                               skip_group_check=True)
                        last = mm(half(bk[2], s), MAT[x][:, s, 2, :], VT[:, s % 2, v], start=False, stop=True,
                                  skip_group_check=True)
                    last.then_inc(ev(f"rhs{x}"), 1)
                elif step < REFINE:
                    lv, second = (step - FIRST_LEVEL + 1) // 2, (step - FIRST_LEVEL) % 2 == 0
                    if not second:
                        pe.wait_ge(ev(f"level{x}"), j * LEVELS + lv)
                        for s in range(4):
                            last = mm(four(bk[2], s), AS[x][:, s, :], GM[x][:, s, :], start=True, stop=True)
                        last.then_inc(ev(f"cross{x}"), 1)
                        return
                    pe.wait_ge(ev(f"crossed{x}"), j * LEVELS + lv + 1)
                    if lv == 0:
                        pe.wait_ge(ev(f"turned_hi{x}"), j + 1)
                    else:
                        pe.wait_ge(ev(f"level_d{x}"), j * (LEVELS - 1) + lv)
                    unit = IDR[:, :].rearrange("p (a t) -> p a t", a=1).broadcast_to([P, 4, T])
                    g_, d_ = (GM[x][:, :, :], DM[x][:, :, :]) if lv else (unit, unit)
                    mm(PS[:, bk[0], :], IDR[:, :], g_, start=True, stop=False, skip_group_check=True)
                    for s in range(4):
                        last = mm(four(bk[0], s), d_[:, s, :], XS[x][:, s, :], start=False, stop=True, skip_group_check=True)
                    last.then_inc(ev(f"update{x}"), 1)
                    if lv < LEVELS - 1:
                        mm(PS[:, bk[1], :], IDR[:, :], d_, start=True, stop=False, skip_group_check=True)
                        for s in range(4):
                            last = mm(four(bk[1], s), XS[x][:, s, :], d_[:, s, :], start=False, stop=True, skip_group_check=True)
                        last.then_inc(ev(f"update_d{x}"), 1)
                elif step < OUTPUT:
                    k_ = step - REFINE
                    if k_ % 2 == 0:
                        src = RSR if k_ == 0 else RR
                        if k_ == 0:
                            pe.wait_ge(ev(f"level{x}"), (j + 1) * LEVELS)
                            pe.wait_ge(ev(f"rhs_hi{x}"), j + 1)
                        else:
                            pe.wait_ge(ev(f"residual{x}"), j * NREF + k_ // 2)
                        for s in range(4):
                            last = mm(half(bk[1], s), GM[x][:, s, :], src[x][:, s, :], start=True, stop=True)
                        last.then_inc(ev(f"solve{x}"), 1)
                    else:
                        pe.wait_ge(ev(f"solved{x}"), j * (NREF + 1) + k_ // 2 + 1)
                        for s in range(4):
                            last = mm(half(bk[2], s), MAT[x][:, s, 0, :], UU[x][:, s, :], start=True, stop=True)
                        last.then_inc(ev(f"product{x}"), 1)
                elif step == OUTPUT:
                    pe.wait_ge(ev(f"solved{x}"), (j + 1) * (NREF + 1))
                    for s in range(4):
                        r = slice(HD * (s // 2), HD * (s // 2) + HD)
                        v = slice((2 * blk + s // 2) * HD, (2 * blk + s // 2 + 1) * HD)
                        o = PS[r, bk[0], (s % 2) * T:(s % 2 + 1) * T]
                        mm(o, UU[x][:, s, :], MAT[x][:, s, 1, :], start=s % 2 == 0, stop=False, skip_group_check=True)
                        last = mm(o, VT[:, s % 2, v], MAT[x][:, s, 3, :], start=False, stop=s % 2 == 0,
                                  skip_group_check=True)
                        if s % 2:
                            last = mm(o, S0P[x][:, s // 2, :], AR[x][:, 1, 1, :], start=False, stop=True,
                                      skip_group_check=True)
                    last.then_inc(ev(f"y_ps{x}"), 1)
                    for a_ in range(2):
                        last = pe.transpose(PS[:, bk[1], a_ * T:(a_ + 1) * T], BKE[x][:, a_, :], IDENT[:, :])
                    last.then_inc(ev(f"bkT{x}"), 1)
                else:
                    pe.wait_ge(ev(f"bk_copied{x}"), j + 1)
                    for hh in range(2):
                        v = slice((2 * blk + hh) * HD, (2 * blk + hh + 1) * HD)
                        c = slice(hh * HD, (hh + 1) * HD)
                        mm(PS[0:HD, bk[2], c], UU[x][:, 2 * hh, :], BKT[x][:, 0, c], start=True, stop=False)
                        last = mm(PS[0:HD, bk[2], c], VT[:, 0, v], BKT[x][:, 1, c], start=False, stop=True)
                    last.then_inc(ev(f"state_ps{x}"), 1)

            def head_sums(src, which, bank):
                for b in range(4):
                    last = mm(PS[:, bank + b // 2, (b % 2) * TOK:(b % 2 + 1) * TOK], HEAD[:, which, :], src[:, b, :],
                              start=True, stop=True)
                return last

            def gn(l, part):
                if part == 0:
                    head_sums(YT, 1, 2).then_inc(ev("gn_ps"), 1)
                    for b in range(4):
                        last = mm(PS[:, 6 + b // 2, (b % 2) * TOK:(b % 2 + 1) * TOK], G2[:, b * P:(b + 1) * P], GLOW,
                                  start=True, stop=True)
                    last.then_inc(ev("gn_ps"), 1)
                elif part == 1:
                    pe.wait_ge(ev("gn_sq"), l + 1)
                    head_sums(TMP, 1, 4).then_inc(ev("gn_ps"), 1)
                else:
                    pe.wait_ge(ev("rk_prod"), l + 1)
                    head_sums(TMP3, 0, 2).then_inc(ev("gn_ps"), 1)

            def sines(l):
                pe.wait_ge(ev("gn_eps"), l + 1)
                mm(PS[0:HID, 4, 0:T], F1[:, :], FEATS[:, :], start=True, stop=True).then_inc(ev("sines_ps"), 1)
                pe.wait_ge(ev("sines_done"), 2 * l + 1)
                mm(PS[0:HID, 5, 0:T], F2[:, :], HD1[:, 0, :], start=True, stop=True).then_inc(ev("sines_ps"), 1)

            def filt(l):
                pe.wait_ge(f3_in, 32 * (l + 1))
                for o in range(4):
                    last = mm(PS[:, 4 + o, :], HD1[:, 1, :], F3[:, o, :], start=True, stop=True)
                last.then_inc(ev("filt_ps"), 1)
                turn_z(l, 0)
                for o in range(2):
                    pe.wait_ge(ev("filt"), 2 * l + o + 1)
                    mm(PS[:, 2 + 3 * o, :], DFT[:, 0, :], HS[:, 2 * o, :], start=True, stop=True)
                    mm(PS[:, 3 + 3 * o, :], DFT[:, 1, :], HS[:, 2 * o, :], start=True, stop=True)
                    mm(PS[:, 4 + 3 * o, :], DFT[:, 2, :], HS[:, 2 * o + 1, :], start=True, stop=True)\
                        .then_inc(ev("spec_ps"), 1)

            def turn_z(l, o):
                for g in range(G):
                    if o:
                        pe.wait_ge(ev("gated"), 2 * l + g + 1)
                    for b in range(4):
                        last = pe.transpose(PS[:, g, b * P:(b + 1) * P], HY[:, b, g * T:(g + 1) * T], IDENT[:, :])
                    last.then_inc(ev("zT_ps"), 1)

            def conv(l, o):
                i = l * 2 + o
                if o:
                    turn_z(l, o)
                else:
                    pe.wait_ge(ev("kf"), 2 * l + 2)
                for g in range(G):
                    pe.wait_ge(ev("zT"), 2 * i + g + 1)
                    mm(PS[:, 4 + 2 * g, :], DFT[:, 0, :], ZT[:, g, :], start=True, stop=True)
                    mm(PS[:, 5 + 2 * g, :], DFT[:, 3, :], ZT[:, g, :], start=True, stop=True).then_inc(ev("zF"), 1)
                for g in range(G):
                    pe.wait_ge(ev("spectrum"), 2 * i + g + 1)
                    for b in range(4):
                        out = PS[:, 2 + g, b * P:(b + 1) * P]
                        mm(out, PAB[:, g, 0, b * P:(b + 1) * P], DFT[:, 4, :], start=True, stop=False)
                        last = mm(out, PAB[:, g, 1, b * P:(b + 1) * P], DFT[:, 5, :], start=False, stop=True)
                    last.then_inc(ev("conv_ps"), 1)

            def merge(l, i):
                if i == 0:
                    pe.wait_ge(ev("yb_lo"), 2 * l + 2)
                for x, (kind, hi, lo) in enumerate((("pa", YAH, YAL), ("pb", YBH, YBL))):
                    n = number[kind, l, i, 0]
                    ready(n)
                    h, s = tile_view(WH, split_no[n] % 2, n), tile_view(WL, split_no[n] % 2, n)
                    for b in range(4):
                        out = PS[:, 4 - 4 * i + 2 * x + b // 2, (b % 2) * TOK:(b % 2 + 1) * TOK]
                        c = slice(b * P, (b + 1) * P)
                        for kb in range(4):
                            mm(out, h[:, kb, c], hi[:, kb, :], start=kb == 0, stop=False)
                            mm(out, h[:, kb, c], lo[:, kb, :], start=False, stop=False)
                            last = mm(out, s[:, kb, c], hi[:, kb, :], start=False, stop=kb == 3)
                    last.then_inc(tile_done, 1)

            def accumulate(n, hi, lo, kb0, nk):
                ready(n)
                k, w = tile_width(n)
                h, s = tile_view(WH, split_no[n] % 2, n), tile_view(WL, split_no[n] % 2, n)
                for j in range(k):
                    for g in range(G):
                        t = slice(g * T, (g + 1) * T)
                        for c in range(2):
                            out = PS[:, 4 + 2 * g + c, :]
                            w_ = slice(c * 512, (c + 1) * 512)
                            f, e_ = kb0[0] == 0, kb0[0] == nk - 1
                            mm(out, hi[:, kb0[1], t], h[:, j, w_], start=f, stop=False)
                            mm(out, lo[:, kb0[1], t], h[:, j, w_], start=False, stop=False)
                            last = mm(out, hi[:, kb0[1], t], s[:, j, w_], start=False, stop=e_)
                    kb0[0] += 1
                    kb0[1] += 1
                last.then_inc(tile_done, 1)

            def gate_rows(l, w):
                if w == 1 and l + 1 < LAYERS:
                    pe.wait_ge(ev("params_read"), l + 2)
                for g in range(G):
                    for b in range(KB):
                        gate = MODT[:, l, (2 + 3 * w) * KB + b, g:g + 1].broadcast_to([P, P])
                        last = mm(PS[:, 2 * g + b // 4, (b % 4) * P:(b % 4 + 1) * P], gate, IDENT[:, :], start=True, stop=True)
                last.then_inc(ev("gate_ps"), 1)

            def out_proj(l):
                at_k = [0, 0]
                for i in range(4):
                    if i % 2 == 0:
                        pe.wait_ge(ev("mg_lo"), 2 * l + i // 2 + 1)
                    if i == 2:
                        gate_rows(l, 0)
                    accumulate(number["o", l, i, 0], MGH, MGL, at_k, 8)

            def ht_done(l, w):
                pe.wait_ge(ev("ht_lo"), 2 * (2 * l + w) + 2)

            def router(l):
                pe.wait_ge(ev("router_lo"), 1)
                for g in range(G):
                    o = PS[:, 2, g * NE:(g + 1) * NE]
                    mm(o, ONES[:, :], RBIAS[0:1, :], start=g == 0, stop=False, skip_group_check=True)
                    for kb in range(KB):
                        t = slice(g * T, (g + 1) * T)
                        mm(o, HTH[:, kb, t], RWH[:, kb, :], start=False, stop=False, skip_group_check=True)
                        mm(o, HTL[:, kb, t], RWH[:, kb, :], start=False, stop=False, skip_group_check=True)
                        last = mm(o, HTH[:, kb, t], RWL[:, kb, :], start=False, stop=kb == KB - 1, skip_group_check=True)
                last.then_inc(ev("router_ps"), 1)

            def spread(l):
                pe.wait_ge(ev("combine"), 1)
                for g in range(G):
                    last = pe.transpose(PS[0:NE, 3, g * T:(g + 1) * T], CMB[:, g, :], IDENT[:, :])
                last.then_inc(ev("router_ps"), 1)
                pe.wait_ge(ev("combT_copied"), 1)
                for e in range(NE):
                    last = mm(PS[:, 4 + e // 2, (e % 2) * TOK:(e % 2 + 1) * TOK], IDENT[0:NE, e:e + 1].broadcast_to([NE, P]), CTT[:, :], start=True, stop=True)
                last.then_inc(ev("router_ps"), 1)

            acc = [0, 0]
            k_bar = 0
            for item in sched:
                what, a = item[0], item[1:]
                if what == "barrier":
                    k_bar += 1
                    pe.wait_ge(act_stage, k_bar)
                    pe.wait_ge(dve_stage, k_bar)
                elif what == "in":
                    product(number["in", a[0], a[1], 0], HTH, HTL)
                elif what == "pair":
                    l, i, e = a
                    product(number["gate", l, i, e], HTH, HTL)
                    product(number["up", l, i, e], HTH, HTL)
                    if l % 2 == 1 and (i, e) == (0, 0):
                        spread(l)
                elif what == "down":
                    l, e = a
                    nk = 22 if l % 2 == 0 else 11
                    total = nk if l % 2 == 0 else nk * NE
                    if e == 0:
                        acc[0] = 0
                    acc[1] = 0 if l % 2 == 0 else 11 * (e % 2)
                    if l % 2 == 1 and e == 0:
                        pe.wait_ge(ev("comb"), 1)
                    for i in range(nk // 2 + nk % 2):
                        pe.wait_ge(ev("pair_lo"), pair_no[l, i, e] + 1)
                        accumulate(number["down", l, i, e], AH, AL, acc, total)
                    if e == (0 if l % 2 == 0 else NE - 1):
                        pe.wait_ge(act_read, act_reads_through(l))
                        pe.wait_ge(dve_read, dve_reads_through(l))
                        gate_rows(l, 1)
                elif what == "part":
                    product(number["in", a[0], a[1], 0], HTH, HTL, a[2], a[3])
                elif what in ("gates", "resid", "z", "affine", "later", "row", "col", "keys", "values"):
                    pass
                else:
                    {"cond": cond, "bias": bias, "consts": consts, "params": params, "ada": ada, "key_norms": key_norms, "turn": turn, "ht": ht, "wprep": wprep, "scan": scan,
                     "gn": gn, "sines": sines, "ht_done": ht_done, "filter": filt, "conv": conv, "merge": merge, "o": out_proj, "router": router}[what](*a)

        @block.scalar
        def _(act):
            steps = Steps(act, sem("act_steps"))
            fn = act.activation

            def make_hi(n):
                if n >= NT or not split(n):
                    return
                m = split_no[n]
                act.wait_ge(ring_in[n % RING], 16 * (n // RING + 1))
                if m >= 2:
                    prev = next(q for q in range(n - 1, -1, -1) if split(q) and split_no[q] == m - 2)
                    act.wait_ge(tile_done, prev + 1)
                k, w = tile_width(n)
                fn(WH[:, m % 2, 0:k * w], WRING[:, n % RING, 0:k * w], ACT.Copy).then_inc(hi_ready, 1)

            def cond():
                act.dma_start(COND[0:8, :], A["c_ctx"].rearrange("(k p) -> k p", p=P)).then_inc(cond_in, 16)
                act.dma_start(COND[8:16, :], A["c"][0].rearrange("(k p) -> k p", p=P)).then_inc(cond_in, 16)
                act.dma_start(IDENT[:, :], A["c_ident"]).then_inc(cond_in, 16)
                act.dma_start(BROW[:, :, :], A["b_ada"].rearrange("l (b p) -> b l p", p=P)).then_inc(bias_in, 16)
                for q, name in enumerate(("ln_g", "ln_b")):
                    for w in range(2):
                        act.dma_start(LNR[(2 * q + w) * KB:(2 * q + w + 1) * KB, :, :],
                                      A[name][:, w, :].rearrange("l (b p) -> b l p", p=P)).then_inc(bias_in, 16)
                act.dma_start(X[:, 0, :], A["x_prompt"][0]).then_inc(x_in, 16)
                act.dma_start(X[:, 1, :], A["x_sample"][0]).then_inc(x_in, 16)
                act.wait_ge(ev("start_ps"), 1)
                steps(fn(CONDT[:, :], PS[:, 2, 0:16], ACT.Silu))
                steps.wait()
                act.sem_inc(ev("cond_silu"), 1)

            def row(l, j):
                n = number["ada", l, j, 0]
                make_hi(n + 2)
                act.wait_ge(tile_done, n + 1)
                if l * ADA + j >= 2:
                    act.wait_ge(ev("ada_turn"), l * ADA + j - 1)
                fn(ADAR[:, j % 2, :], PS[0:2, bank_of[n], 0:256], ACT.Copy).then_inc(ev("ada_row"), 1)

            def mod_columns(l, w):
                return 3 * w * 8, (3 * w + 1) * 8

            def ht(l, w, g):
                shift, scale = mod_columns(l, w)
                act.wait_ge(ev("xT"), (2 * l + w) * 4 + 2 * g + 1)
                t = slice(g * T, (g + 1) * T)
                for kb in range(4):
                    steps(fn(HTF[:, kb, t], PS[:, 2 + 2 * g, kb * P:(kb + 1) * P], ACT.Identity,
                             bias=MODT[:, l, shift + kb, g:g + 1], scale=MODT[:, l, scale + kb, g:g + 1]))
                steps.wait()
                fn(HTH[:, 0:4, t], HTF[:, 0:4, t], ACT.Copy).then_inc(ev("ht_hi"), 1)
                steps.wait_for(ev("ht_hi"), 2 * (2 * l + w) + g + 1)
                if l == 1 and w == 1 and g == 1:
                    fn(RWH[:, :, :], RW_[:, :, :], ACT.Copy).then_inc(ev("router_hi"), 1)

            def ht_done(l, w):
                if l + w:
                    make_hi(behind_norm(2 * l + w - 1))
                steps.wait()

            def mixed(l, i):
                n = number["in", l, i, 0]
                make_hi(n + 2)
                act.wait_ge(tile_done, n + 1)
                for x, b in enumerate(in_blocks(i)):
                    src = PS[:, bank_of[n], x * TOK:(x + 1) * TOK]
                    if b < RB:
                        last = fn(RW[:, b, :], src, ACT.Identity, scale=CEN[:, b:b + 1])
                    elif b < RB + HB:
                        c = b - RB
                        last = fn(HY[:, c, :], src, ACT.Identity, scale=PT[:, ROW_AT["cw1"] + c:ROW_AT["cw1"] + c + 1],
                                  bias=PT[:, ROW_AT["cb"] + c:ROW_AT["cb"] + c + 1])
                    else:
                        last = fn(SG[:, b - RB - HB, :], src, ACT.Sigmoid)
                if i < 14:
                    last.then_inc(ev("center"), 1)
                    steps.wait_for(ev("center"), l * 14 + i + 1)
                else:
                    last.then_inc(act_read, 1)
                    steps.wait_for(act_read, read_no[n])

            def key_norms(l):
                act.wait_ge(ev("kk_max"), l + 1)
                fn(TMP2[:, :, :], TMP2[:, :, :], ACT.Sqrt).then_inc(ev("kk_root"), 1)
                steps.wait_for(ev("kk_root"), l + 1)

            def wprep(l):
                act.wait_ge(ev("values"), l + 1)
                fn(WLOW, WLOW, ACT.Tanh).then_inc(ev("wlow"), 1)
                for x in range(4):
                    act.wait_ge(ev("w_pre"), l * 4 + x + 1)
                    fn(SGW[:, x, :], PS[:, 2 + x, :], ACT.Sigmoid).then_inc(ev("sgw"), 1)
                for g in range(G):
                    act.wait_ge(ev("vT"), l * 2 + g + 1)
                    steps(fn(VT[:, g, :], PS[:, 6 + g, :], ACT.Copy))
                act.wait_ge(ev("glow"), l + 1)
                steps(fn(GLOW, GLOW, ACT.Sigmoid))
                act.wait_ge(ev("s0T"), l + 1)
                steps(fn(S0T[:, :, :], PS[:, 4, :].rearrange("p (a b) -> p a b", a=8), ACT.Copy))
                act.wait_ge(ev("sgw"), 4 * (l + 1))

            def scan(l, b, step):
                i, blk, d = l * 8 + b, b // 2, b % 2
                j, x = l * 4 + blk, d
                bk = [2 + 3 * x, 3 + 3 * x, 4 + 3 * x]
                four = lambda bank: PS[:, bank, :].rearrange("p (a t) -> p a t", a=4)
                if step == 0:
                    act.wait_ge(ev(f"decay_sum{x}"), j + 1)
                    if blk:
                        act.wait_ge(ev(f"y_ps{x}"), j)
                    o = PS[:, bk[0], 0:258].rearrange("p (g t) -> p g t", g=2)
                    c = d * 4 + blk
                    fn(AA[x][:, :], PS[:, bk[1], 0:TOK], ACT.Tanh, bias=A0H[:, c:c + 1], scale=0.5)
                    fn(EX[x][:, :, :], o, ACT.Exp, scale=-DECAY_SCALE)
                    fn(EI[x][:, :, :], o, ACT.Exp, scale=DECAY_SCALE).then_inc(ev(f"decays{x}"), 1)
                elif step == 3:
                    act.wait_ge(ev(f"turned{x}"), j + 1)
                    act.wait_ge(ev(f"ends{x}"), j + 1)
                    fn(AS[x][:, :, :], four(bk[1]), ACT.Copy).then_inc(ev(f"turned_hi{x}"), 1)
                    act.wait_ge(ev(f"rhs_copied{x}"), j + 1)
                    fn(RSR[x][:, :, :], RS[x][:, :, :], ACT.Copy).then_inc(ev(f"rhs_hi{x}"), 1)
                elif FIRST_LEVEL <= step < REFINE and (step - FIRST_LEVEL) % 2 == 0:
                    lv = (step - FIRST_LEVEL) // 2
                    act.wait_ge(ev(f"update{x}"), j * LEVELS + lv + 1)
                    fn(GM[x][:, :, :], four(bk[0]), ACT.Copy).then_inc(ev(f"level{x}"), 1)
                    if lv < LEVELS - 1:
                        act.wait_ge(ev(f"update_d{x}"), j * (LEVELS - 1) + lv + 1)
                        fn(DM[x][:, :, :], four(bk[1]), ACT.Copy).then_inc(ev(f"level_d{x}"), 1)
                elif step == OUTPUT:
                    act.wait_ge(ev(f"bkT{x}"), j + 1)
                    fn(BKT[x][:, :, :], PS[:, bk[1], 0:2 * T].rearrange("p (a t) -> p a t", a=2), ACT.Copy)\
                        .then_inc(ev(f"bk_copied{x}"), 1)
                elif step == OUTPUT + 1:
                    act.wait_ge(ev(f"state_ps{x}"), j + 1)
                    fn(SFS[x][:, :, :], PS[0:HD, bk[2], 0:P].rearrange("p (a t) -> p a t", a=2), ACT.Copy)\
                        .then_inc(ev(f"state_copied{x}"), 1)
                    act.wait_ge(ev(f"state_copied{x}"), j + 1)
                    act.dma_start(new_state[0, l, d, 2 * blk:2 * blk + 2].rearrange("h v k -> v h k"), SFS[x][:, :, :])\
                        .then_inc(ev(f"state_out{x}"), 16)

            def gn(l, part):
                if part == 0:
                    act.wait_ge(ev("gn_cent"), l + 1)
                    fn(TMP[:, :, :], YT[:, :, :], ACT.Square).then_inc(ev("gn_sq"), 1)
                elif part == 1:
                    act.wait_ge(ev("gn_eps"), l + 1)
                    fn(TMP2[:, :, :], TMP2[:, :, :], ACT.Sqrt).then_inc(ev("gn_root"), 1)
                else:
                    act.wait_ge(ev("ya"), l + 1)
                    fn(YAH[:, :, :], YT[:, :, :], ACT.Copy).then_inc(ev("ya_hi"), 1)
                    steps.wait_for(ev("ya_hi"), l + 1)

            def sines(l):
                act.wait_ge(ev("sines_arg"), 2 * l + 1)
                fn(HD1[:, 0, :], HDT[:, 0, :], ACT.Sin).then_inc(ev("sines_done"), 1)
                act.wait_ge(ev("sines_arg"), 2 * l + 2)
                fn(HD1[:, 1, :], HDT[:, 0, :], ACT.Sin).then_inc(ev("sines_done"), 1)
                steps.wait_for(ev("sines_done"), 2 * l + 2)

            def filt(l):
                copy_z(l, 0)
                for o in range(2):
                    act.wait_ge(ev("spec_ps"), 2 * l + o + 1)
                    fn(KF[:, o, :, :], PS[:, 2 + 3 * o:5 + 3 * o, :], ACT.Copy).then_inc(ev("kf"), 1)

            def copy_z(l, o):
                for g in range(G):
                    act.wait_ge(ev("zT_ps"), 2 * (2 * l + o) + g + 1)
                    fn(ZT[:, g, :], PS[:, g, :], ACT.Copy).then_inc(ev("zT"), 1)

            def conv(l, o):
                if o == 0:
                    copy_z(l, 1)
                else:
                    for g in range(G):
                        t = slice(g * T, (g + 1) * T)
                        act.wait_ge(ev("yb"), 2 * l + g + 1)
                        fn(YBH[:, :, t], HY[:, 0:4, t], ACT.Copy).then_inc(ev("yb_hi"), 1)

            def merge(l, i):
                make_hi(number["pa", l, i, 0] + 2)
                make_hi(number["pb", l, i, 0] + 2)
                act.wait_ge(ev("merged"), 4 * (l * 2 + i) + 4)
                fn(MGH[:, 4 * i:4 * i + 4, :], MG[:, 4 * i:4 * i + 4, :], ACT.Copy).then_inc(ev("mg_hi"), 1)
                act.wait_ge(ev("mg_hi"), l * 2 + i + 1)

            def gates(l, w):
                if w == 0:
                    for j in range(3):
                        make_hi(number["o", l, j, 0] + 2)
                act.wait_ge(ev("gate_ps"), l * 2 + w + 1)
                fn(GBC[:, :, :].rearrange("p g (c n) -> p (g c) n", c=2), PS[:, 0:4, :], ACT.Copy).then_inc(ev("gate_rows"), 1)

            def resid(l, w, g):
                act.wait_ge(ev("var"), (l * 2 + w) * 2 + g + 1)
                fn(MV[:, g, 2:3], MV[:, g, 1:2], ACT.Sqrt).then_inc(ev("std"), 1)

            def z(l, w, g):
                act.wait_ge(ev("rstd"), (l * 2 + w) * 2 + g + 1)
                fn(X[:, g, :], X[:, g, :], ACT.Identity, scale=MV[:, g, 3:4], bias=MV[:, g, 0:1]).then_inc(ev("z"), 1)
                steps.wait_for(ev("z"), (l * 2 + w) * 2 + g + 1)

            def router(l):
                act.wait_ge(ev("shifted"), 1)
                fn(PR[:, :, :], LG[:, :, :], ACT.Exp).then_inc(ev("exps"), 1)
                act.wait_ge(ev("router_ps"), 2)
                fn(CTT[:, :], PS[0:NE, 3, 0:TOK], ACT.Copy).then_inc(ev("combT_copied"), 1)
                act.wait_ge(ev("router_ps"), 3)
                fn(CB[:, :, :].rearrange("p (a b) t -> p a (b t)", a=4), PS[:, 4:8, :], ACT.Copy).then_inc(ev("comb"), 1)

            def pair(l, i, e):
                n = number["gate", l, i, e]
                make_hi(n + 2)
                act.wait_ge(tile_done, n + 1)
                u = pair_no[l, i, e]
                k, w = tile_width(n)
                if u >= 2:
                    act.wait_ge(ev("pair_lo"), u - 1)
                fn(SL[:, u % 2, 0:w // P, :], PS[:, bank_of[n], 0:w * 2].rearrange("p (b t) -> p b t", t=TOK), ACT.Silu)\
                    .then_inc(act_read, 1)
                make_hi(n + 3)
                if i == 0 and l % 2 == 1 and e >= 2:
                    act.wait_ge(tile_done, number["down", l, 5, e - 2] + 1)
                act.wait_ge(ev("hidden"), u + 1)
                o = (0 if l % 2 == 0 else 11 * (e % 2)) + 2 * i
                fn(AH[:, o:o + w // P, :], SL[:, u % 2, 0:w // P, :], ACT.Copy).then_inc(ev("pair_hi"), 1)
                act.wait_ge(ev("pair_hi"), u + 1)

            def down(l, e):
                cnt = 11 if l % 2 == 0 else 6
                for i in range(cnt):
                    if number["down", l, i, e] + 2 != behind_norm(2 * l + 1):
                        make_hi(number["down", l, i, e] + 2)

            k_bar = 0
            for item in sched:
                what, a = item[0], item[1:]
                if what == "barrier":
                    k_bar += 1
                    steps.wait()
                    act.sem_inc(act_stage, 1)
                    act.wait_ge(dve_stage, k_bar)
                elif what in ("bias", "keys", "values", "consts", "params", "part", "ada", "turn", "col", "affine"):
                    pass
                elif what in ("in", "later"):
                    mixed(*a)
                elif what == "o":
                    pass
                else:
                    {"cond": cond, "row": row, "ht": ht, "ht_done": ht_done, "key_norms": key_norms, "wprep": wprep,
                     "scan": scan, "gn": gn, "sines": sines, "filter": filt, "conv": conv, "merge": merge,
                     "gates": gates, "resid": resid, "z": z, "router": router, "pair": pair, "down": down}[what](*a)

        @block.vector
        def _(dve):
            steps = Steps(dve, sem("dve_steps"))
            tt, ts, stt = dve.tensor_tensor, dve.tensor_scalar, dve.scalar_tensor_tensor

            def param(name, b):
                return PT[:, ROW_AT[name] + b:ROW_AT[name] + b + 1]

            def make_lo(n):
                if n >= NT or not split(n):
                    return
                m = split_no[n]
                dve.wait_ge(hi_ready, m + 1)
                k, w = tile_width(n)
                tt(WL[:, m % 2, 0:k * w], WRING[:, n % RING, 0:k * w], WH[:, m % 2, 0:k * w].bitcast(F32), ALU.subtract)\
                    .then_inc(lo_ready, 1)

            def bias():
                dve.wait_ge(ev("start_ps"), 2)
                for x in range(LAYERS):
                    steps(dve.tensor_copy(BADT[:, x, :], PS[:, 4, 64 * x:48 + 64 * x]))
                    steps(dve.tensor_copy(LNT[:, x, :], PS[:, 4, 128 + 32 * x:160 + 32 * x]))
                steps.wait()
                for c in (8, 32):
                    steps(ts(BADT[:, :, c:c + 8], BADT[:, :, c:c + 8], 1.0, None, ALU.add))

            def consts():
                dve.wait_ge(x_in, 32)
                dve.wait_ge(const_in, NCONST)
                steps(tt(X[:, 1, :], X[:, 1, :], POS[:, :], ALU.add))
                steps(dve.tensor_copy(MASKS[:, :, :, :], MASKF[:, :, :, :]))
                steps(dve.tensor_copy(LEVEL[:, :, :, :], LEVELF[:, :, :, :]))
                steps(dve.tensor_copy(IDR[:, :], IDENT[:, :]))

            def params(l):
                dve.wait_ge(ev("paramT"), l + 1)
                steps(dve.tensor_copy(PT[:, :], PS[:, 3, 0:NROW]))
                steps.wait()
                dve.sem_inc(ev("params_read"), 1)
                steps(tt(CEN[:, :], PT[:, 0:RB], PT[:, ROW_AT["mu1"]:ROW_AT["mu1"] + RB], ALU.add))
                steps(ts(KAH[:, :], PT[:, ROW_AT["ka"]:ROW_AT["ka"] + 4], 0.5, None, ALU.mult))
                steps(ts(KAM[:, :], PT[:, ROW_AT["ka"]:ROW_AT["ka"] + 4], -0.5, 1.0, ALU.mult, ALU.add))
                steps(ts(A0H[:, :], PT[:, ROW_AT["a0"]:ROW_AT["a0"] + 8], 0.5, None, ALU.mult))
                steps.wait()
                steps(ts(CEN[:, :], CEN[:, :], -1.0, 1.0, ALU.mult, ALU.add))

            def col(l, j):
                n = number["ada", l, j, 0]
                dve.wait_ge(ev("ada_turn"), l * ADA + j + 1)
                c = slice(2 * j, 2 * j + 2)
                bias = BADT[:, l, c].rearrange("p (b a) -> p b a", a=1).broadcast_to([P, 2, 2])
                if j == 0:
                    steps.wait()
                tt(MODT[:, l, c, :], PS[:, bank_of[n], 256:260].rearrange("p (b c) -> p b c", c=2), bias, ALU.add)\
                    .then_inc(dve_read, 1)
                steps.wait_for(dve_read, read_no[n])

            def ht(l, w, g):
                shift, scale = 3 * w * KB, (3 * w + 1) * KB
                dve.wait_ge(ev("xT"), (2 * l + w) * 4 + 2 * g + 2)
                t = slice(g * T, (g + 1) * T)
                for kb in range(4, 8):
                    steps(ts(HTF[:, kb, t], PS[:, 3 + 2 * g, (kb - 4) * P:(kb - 3) * P], MODT[:, l, scale + kb, g:g + 1],
                             MODT[:, l, shift + kb, g:g + 1], ALU.mult, ALU.add))
                steps.wait()
                steps(dve.tensor_copy(HTH[:, 4:8, t], HTF[:, 4:8, t]))
                steps.wait()
                dve.wait_ge(ev("ht_hi"), 2 * (2 * l + w) + g + 1)
                tt(HTL[:, :, t], HTF[:, :, t], HTH[:, :, t].bitcast(F32), ALU.subtract).then_inc(ev("ht_lo"), 1)
                steps.wait_for(ev("ht_lo"), 2 * (2 * l + w) + g + 1)
                if l == 1 and w == 1 and g == 1:
                    dve.wait_ge(ev("router_hi"), 1)
                    tt(RWL[:, :, :], RW_[:, :, :], RWH[:, :, :].bitcast(F32), ALU.subtract).then_inc(ev("router_lo"), 1)

            def ht_done(l, w):
                if l + w:
                    make_lo(behind_norm(2 * l + w - 1))
                steps.wait()

            def mixed(l, i):
                n = number["in", l, i, 0]
                make_lo(n + 2)
                if i >= 14:
                    return
                dve.wait_ge(ev("center"), l * 14 + i + 1)
                for side in range(2):
                    for x, b in enumerate(in_blocks(i)):
                        src = PS[:, bank_of[n], x * TOK:(x + 1) * TOK].rearrange("p (g t) -> p g t", g=G)
                        dst = RW[:, b, :] if b < RB else HY[:, b - RB, :]
                        dst = dst.rearrange("p (g t) -> p g t", g=G)
                        o, s = (dst[:, :, 1:T], src[:, :, 0:T - 1]) if side == 0 else (dst[:, :, 0:T - 1], src[:, :, 1:T])
                        c = b + side * (RB + HB)
                        last = stt(o, s, PT[:, c:c + 1], o, ALU.mult, ALU.add)
                        if side == 1 and x == len(in_blocks(i)) - 1:
                            last.then_inc(dve_read, 1)
                            steps.wait_for(dve_read, read_no[n])
                        else:
                            steps(last)
                    if side == 0:
                        steps.wait()

            def keys(l):
                steps.wait()
                for b in range(4):
                    steps(ts(KK[:, b, :], RW[:, 4 + b, :], param("kk", b), None, ALU.mult))
                steps.wait()
                tt(TMP[:, :, :], KK[:, :, :], KK[:, :, :], ALU.mult).then_inc(ev("kk_sq"), 1)

            def key_norms(l):
                dve.wait_ge(ev("kk_norm"), l + 1)
                ts(TMP2[:, :, :].rearrange("p (a b) t -> p a (b t)", a=2), PS[:, 2:4, :], 1e-24, None, ALU.max)\
                    .then_inc(ev("kk_max"), 1)
                steps.wait_for(ev("kk_max"), l + 1)

            def values(l):
                steps.wait()
                dve.sem_inc(ev("values"), 1)

            def wprep(l):
                steps.wait()
                dve.sem_inc(ev("glow"), 1)
                dve.wait_ge(ev("kk_root"), l + 1)
                steps(dve.reciprocal(TMP2[:, :, :], TMP2[:, :, :]))
                steps.wait()
                tt(KK[:, :, :], KK[:, :, :], TMP2[:, :, :], ALU.mult).then_inc(ev("kk_done"), 1)
                steps.wait_for(ev("kk_done"), l + 1)

            def scan(l, b, step):
                i, blk, d = l * 8 + b, b // 2, b % 2
                j, x = l * 4 + blk, d
                bk = [2 + 3 * x, 3 + 3 * x, 4 + 3 * x]
                q4 = lambda m: m.rearrange("p (a t) -> p a t", a=1).broadcast_to([P, 4, T])
                flat = lambda t_: t_.rearrange("p a n -> p (a n)")
                if step == 0:
                    ex, ei, t2 = EX[x], EI[x], T2[x]
                    own, before = (1, 0) if d == 0 else (0, 1)
                    at_ = lambda e_, o: e_[:, :, o:o + T]
                    g3 = lambda v: v.rearrange("p (g t) -> p g t", g=G)
                    if blk:
                        dve.wait_ge(ev(f"state_ps{x}"), j)
                    dve.wait_ge(ev(f"decays{x}"), j + 1)
                    steps(stt(t2[:, :], AA[x][:, :], 1.0, KK[:, blk, :], ALU.add, ALU.mult))
                    steps(stt(AR[x][:, :, 0, :], g3(KK[:, blk, :]), -1.0, at_(ex, before), ALU.mult, ALU.mult))
                    steps(tt(AR[x][:, :, 1, :], g3(RW[:, blk, :]), at_(ex, own), ALU.mult))
                    steps.wait()
                    stt(BK[x][:, 0, :, :], g3(t2[:, :]), 0.5, at_(ei, own), ALU.mult, ALU.mult)\
                        .then_inc(ev(f"factors{x}"), 1)
                    steps.wait_for(ev(f"factors{x}"), j + 1)
                    if blk == 0:
                        dve.wait_ge(ev("zeros"), 4 * l + 2)
                    start = 0 if d == 0 else T
                    for hh in range(2):
                        r = slice(HD * hh, HD * hh + HD)
                        steps(ts(S0P[x][r, hh, :], S0T[r, d * 4 + blk, :], EI[x][r, 1, start:start + 1], None, ALU.mult))
                    steps.wait()
                elif step in (1, 2):
                    if step == 1 and blk == 0:
                        dve.wait_ge(ev("zeros"), 4 * l + 4)
                    for s in ((0, 1, 2) if step == 1 else (3,)):
                        dve.wait_ge(ev(f"gram{x}"), 4 * j + s + 1)
                        dve.copy_predicated(MAT[x][:, s, :, :].rearrange("p m t -> p (m t)"),
                                            MASKS[:, d, :, :].rearrange("p m t -> p (m t)"), PS[:, bk[s % 3], :])\
                            .then_inc(ev(f"masked{x}"), 1)
                elif step == 3:
                    dve.wait_ge(ev(f"masked{x}"), 4 * j + 4)
                    dve.wait_ge(ev(f"ends{x}"), j + 1)
                    tt(XS[x][:, :, :], MAT[x][:, :, 0, :], q4(LEVEL[:, d, 0, :]), ALU.mult).then_inc(ev(f"crossed{x}"), 1)
                    dve.wait_ge(ev(f"rhs{x}"), j + 1)
                    if j:
                        dve.wait_ge(ev(f"state_out{x}"), 16 * j)
                    dve.tensor_copy(flat(RS[x][:, :, :]), PS[:, bk[2], 0:4 * HD]).then_inc(ev(f"rhs_copied{x}"), 1)
                elif FIRST_LEVEL <= step < REFINE:
                    lv = (step - FIRST_LEVEL + 1) // 2
                    if (step - FIRST_LEVEL) % 2:
                        dve.wait_ge(ev(f"cross{x}"), j * (LEVELS - 1) + lv)
                        tt(XS[x][:, :, :], PS[:, bk[2], :].rearrange("p (a t) -> p a t", a=4), q4(LEVEL[:, d, lv, :]),
                           ALU.mult).then_inc(ev(f"crossed{x}"), 1)
                elif step < OUTPUT:
                    k_ = step - REFINE
                    if k_ == 0:
                        dve.wait_ge(ev(f"solve{x}"), j * (NREF + 1) + 1)
                        dve.tensor_copy(flat(UU[x][:, :, :]), PS[:, bk[1], 0:4 * HD]).then_inc(ev(f"solved{x}"), 1)
                        dve.wait_ge(ev(f"solved{x}"), j * (NREF + 1) + 1)
                    elif k_ % 2:
                        steps(tt(BKW[x][:, :, :], RS[x][:, :, :], UU[x][:, :, :], ALU.subtract))
                        steps.wait()
                        dve.wait_ge(ev(f"product{x}"), j * NREF + k_ // 2 + 1)
                        tt(flat(RR[x][:, :, :]), flat(BKW[x][:, :, :]), PS[:, bk[2], 0:4 * HD], ALU.add)\
                            .then_inc(ev(f"residual{x}"), 1)
                    else:
                        dve.wait_ge(ev(f"solve{x}"), j * (NREF + 1) + k_ // 2 + 1)
                        tt(flat(UU[x][:, :, :]), flat(UU[x][:, :, :]), PS[:, bk[1], 0:4 * HD], ALU.add)\
                            .then_inc(ev(f"solved{x}"), 1)
                        dve.wait_ge(ev(f"solved{x}"), j * (NREF + 1) + k_ // 2 + 1)
                elif step == OUTPUT:
                    dve.wait_ge(ev(f"y_ps{x}"), j + 1)
                    src = PS[:, bk[0], 0:TOK]
                    if d == 0:
                        dve.tensor_copy(YT[:, blk, :], src).then_inc(ev(f"y_added{x}"), 1)
                    else:
                        dve.wait_ge(ev("y_added0"), j + 1)
                        tt(YT[:, blk, :], YT[:, blk, :], src, ALU.add).then_inc(ev(f"y_added{x}"), 1)
                    if b >= 6:
                        dve.wait_ge(ev(f"y_added{x}"), j + 1)

            def gn(l, part):
                two = lambda x: x.rearrange("p (a b) t -> p a (b t)", a=2)
                if part == 0:
                    for x in range(2):
                        dve.wait_ge(ev(f"state_out{x}"), 16 * 4 * (l + 1))
                    dve.wait_ge(ev("gn_ps"), 4 * l + 1)
                    tt(two(YT[:, :, :]), two(YT[:, :, :]), PS[:, 2:4, :], ALU.subtract).then_inc(ev("gn_cent"), 1)
                    steps(tt(TMP3[:, :, :], RW[:, 0:4, :], KS, ALU.mult))
                    steps.wait()
                    for b in range(4):
                        last = ts(TMP3[:, b, :], TMP3[:, b, :], param("rk", b), 0.5, ALU.mult, ALU.mult)
                        if b < 3:
                            steps(last)
                    last.then_inc(ev("rk_prod"), 1)
                    steps.wait_for(ev("rk_prod"), l + 1)
                elif part == 1:
                    dve.wait_ge(ev("gn_ps"), 4 * l + 3)
                    ts(two(TMP2[:, :, :]), PS[:, 4:6, :], GN_EPS, None, ALU.add).then_inc(ev("gn_eps"), 1)
                    dve.wait_ge(ev("gn_root"), l + 1)
                    steps(dve.reciprocal(TMP2[:, :, :], TMP2[:, :, :]))
                    steps.wait()
                    steps(tt(YT[:, :, :], YT[:, :, :], TMP2[:, :, :], ALU.mult))
                else:
                    dve.wait_ge(ev("gn_ps"), 4 * l + 4)
                    steps(tt(two(TMP[:, :, :]), PS[:, 2:4, :], two(RW[:, 8:12, :]), ALU.mult))
                    steps.wait()
                    for b in range(4):
                        steps(ts(YT[:, b, :], YT[:, b, :], param("gw", b), param("gb", b), ALU.mult, ALU.add))
                    steps.wait()
                    steps(tt(YT[:, :, :], YT[:, :, :], TMP[:, :, :], ALU.add))
                    steps.wait()
                    dve.wait_ge(ev("gn_ps"), 4 * l + 2)
                    tt(two(YT[:, :, :]), two(YT[:, :, :]), PS[:, 6:8, :], ALU.mult).then_inc(ev("ya"), 1)
                    dve.wait_ge(ev("ya_hi"), l + 1)
                    steps(tt(YAL[:, :, :], YT[:, :, :], YAH[:, :, :].bitcast(F32), ALU.subtract))

            def sine_argument(bank, c, mark):
                big, two_pi = 12582912.0, 2 * math.pi
                hi_part = 6.28125
                x, k_ = HDT[:, 0, :], HDT[:, 1, :]
                steps(ts(x, PS[0:HID, bank, 0:T], FB[:, c:c + 1], None, ALU.add))
                steps.wait()
                steps(ts(k_, x, 1 / two_pi, big, ALU.mult, ALU.add))
                steps.wait()
                steps(ts(k_, k_, -big, None, ALU.add))
                steps.wait()
                steps(stt(x, k_, -hi_part, x, ALU.mult, ALU.add))
                steps.wait()
                steps(stt(x, k_, -(two_pi - hi_part), x, ALU.mult, ALU.add))
                steps.wait()
                ts(x, x, math.pi - 2e-7, -(math.pi - 2e-7), ALU.min, ALU.max).then_inc(mark, 1)

            def sines(l):
                dve.wait_ge(ev("sines_ps"), 2 * l + 1)
                sine_argument(4, 0, ev("sines_arg"))
                dve.wait_ge(ev("sines_ps"), 2 * l + 2)
                sine_argument(5, 1, ev("sines_arg"))
                steps.wait_for(ev("sines_arg"), 2 * l + 2)

            def filt(l):
                dve.wait_ge(ev("filt_ps"), l + 1)
                for o in range(2):
                    f, b = HS[:, 2 * o, :], HS[:, 2 * o + 1, :]
                    for q, h in enumerate((f, b)):
                        steps(tt(h, PS[:, 4 + 2 * o + q, :], WINDOW[:, q, :], ALU.mult))
                    steps.wait()
                    steps(tt(f, f, b, ALU.add))
                    steps.wait()
                    stt(b, b, 2.0, f, ALU.mult, ALU.subtract).then_inc(ev("filt"), 1)

            def conv(l, o):
                i = l * 2 + o
                kr, krb, ki = KF[:, o, 0, :], KF[:, o, 1, :], KF[:, o, 2, :]
                for g in range(G):
                    dve.wait_ge(ev("zF"), i * 2 + g + 1)
                    zr, zi = PS[:, 4 + 2 * g, :], PS[:, 5 + 2 * g, :]
                    steps(tt(PAB[:, g, 0, :], zr, kr, ALU.mult))
                    steps(tt(CT1[:, g, :], zi, ki, ALU.mult))
                    steps(tt(PAB[:, g, 1, :], zr, ki, ALU.mult))
                    steps(tt(CT2[:, g, :], zi, krb, ALU.mult))
                    steps.wait()
                    steps(tt(PAB[:, g, 0, :], PAB[:, g, 0, :], CT1[:, g, :], ALU.subtract))
                    tt(PAB[:, g, 1, :], PAB[:, g, 1, :], CT2[:, g, :], ALU.add).then_inc(ev("spectrum"), 1)
                    steps.wait_for(ev("spectrum"), i * 2 + g + 1)
                for g in range(G):
                    t = slice(g * T, (g + 1) * T)
                    dve.wait_ge(ev("conv_ps"), i * 2 + g + 1)
                    for b in range(4):
                        steps(stt(HY[:, b, t], HY[:, b, t], param("sk", o * 4 + b), PS[:, 2 + g, b * P:(b + 1) * P],
                                  ALU.mult, ALU.add))
                    steps.wait()
                    mark = ev("gated" if o == 0 else "yb")
                    tt(HY[:, 0:4, t], HY[:, 0:4, t], HY[:, 4 + 4 * o:8 + 4 * o, t], ALU.mult).then_inc(mark, 1)
                    steps.wait_for(mark, 2 * l + g + 1)
                for g in range(G if o else 0):
                    t = slice(g * T, (g + 1) * T)
                    dve.wait_ge(ev("yb_hi"), 2 * l + g + 1)
                    steps.wait()
                    tt(YBL[:, :, t], HY[:, 0:4, t], YBH[:, :, t].bitcast(F32), ALU.subtract).then_inc(ev("yb_lo"), 1)

            def merge(l, i):
                make_lo(number["pa", l, i, 0] + 2)
                make_lo(number["pb", l, i, 0] + 2)
                dve.wait_ge(tile_done, number["pb", l, i, 0] + 1)
                two = lambda x: x.rearrange("p b t -> p (b t)")
                for x in range(2):
                    b = 4 * i + 2 * x
                    steps(tt(two(MG[:, b:b + 2, :]), PS[:, 4 - 4 * i + x, :], two(SG[:, b:b + 2, :]), ALU.mult))
                    steps(tt(two(MGT[:, :, :]), PS[:, 6 - 4 * i + x, :], two(SG[:, 8 + b:10 + b, :]), ALU.mult))
                    steps.wait()
                    tt(MG[:, b:b + 2, :], MG[:, b:b + 2, :], MGT[:, :, :], ALU.add).then_inc(ev("merged"), 2)
                    dve.wait_ge(ev("merged"), 4 * (l * 2 + i) + 2 * x + 2)
                dve.wait_ge(ev("mg_hi"), l * 2 + i + 1)
                q = slice(4 * i, 4 * i + 4)
                tt(MGL[:, q, :], MG[:, q, :], MGH[:, q, :].bitcast(F32), ALU.subtract).then_inc(ev("mg_lo"), 1)

            def gates(l, w):
                if w == 0:
                    for j in range(3):
                        make_lo(number["o", l, j, 0] + 2)
                if 2 * l + w < 2 * LAYERS - 1:
                    m, v = divmod(2 * l + w + 1, 2)
                    both = lambda c: LNT[:, l, c:c + KB].rearrange("p (b a) -> p b a", a=1).broadcast_to([P, KB, 2])
                    shift, scale = (MODT[:, m, (3 * v + q) * KB:(3 * v + q + 1) * KB, :] for q in range(2))
                    steps.wait()
                    steps(tt(FOLD[:, :, :], scale, both((2 + w) * KB), ALU.mult))
                    steps.wait()
                    steps(tt(shift, shift, FOLD[:, :, :], ALU.add))
                    steps(tt(scale, scale, both(w * KB), ALU.mult))
                steps.wait()
                if w == 0:
                    last_tile = number["o", l, 3, 0]
                else:
                    last_tile = number["down", l, 10, 0] if l % 2 == 0 else number["down", l, 5, NE - 1]
                dve.wait_ge(tile_done, last_tile + 1)
                dve.wait_ge(ev("gate_rows"), l * 2 + w + 1)

            def resid(l, w, g):
                i = l * 2 + w
                gb = GBC[:, g, :].rearrange("p (c n) -> p c n", c=2)
                xg = X[:, g, :]
                steps(tt(gb, PS[:, 4 + 2 * g:6 + 2 * g, :], gb, ALU.mult))
                steps.wait()
                steps(stt(xg, xg, ALPHA, GBC[:, g, :], ALU.mult, ALU.add))
                steps.wait()
                for c in range(2):
                    steps(dve.bn_stats(STAT[:, g, 6 * c:6 * c + 6], xg[:, c * 512:(c + 1) * 512]))
                steps.wait()
                steps(dve.bn_aggr(MV[:, g, 0:2], STAT[:, g, :]))
                steps.wait()
                ts(MV[:, g, 1:2], MV[:, g, 1:2], LN_EPS, None, ALU.add).then_inc(ev("var"), 1)
                dve.wait_ge(ev("std"), i * 2 + g + 1)
                steps(dve.reciprocal(MV[:, g, 3:4], MV[:, g, 2:3]))
                steps.wait()
                stt(MV[:, g, 0:1], MV[:, g, 0:1], -1.0, MV[:, g, 3:4], ALU.mult, ALU.mult).then_inc(ev("rstd"), 1)
                steps.wait_for(ev("rstd"), i * 2 + g + 1)

            def affine(l, w):
                i = l * 2 + w
                dve.wait_ge(lngb_in, 32 * (i + 1))
                for g in range(G):
                    dve.wait_ge(ev("z"), 2 * i + g + 1)
                    steps(tt(X[:, g, :], X[:, g, :], LNGB[:, 0, :], ALU.mult))
                    steps.wait()
                    tt(X[:, g, :], X[:, g, :], LNGB[:, 1, :], ALU.add).then_inc(ev("affine"), 1)
                steps.wait_for(ev("affine"), 2 * i + 2)

            def router(l):
                e3 = lambda x: x.broadcast_to([P, G, NE])
                dve.wait_ge(ev("router_ps"), 1)
                lg = PS[:, 2, 0:G * NE].rearrange("p (g e) -> p g e", g=G)
                steps(dve.tensor_reduce(SM[:, :, 0:1], lg, AX.X, ALU.max))
                steps.wait()
                tt(LG[:, :, :], lg, e3(SM[:, :, 0:1]), ALU.subtract).then_inc(ev("shifted"), 1)
                dve.wait_ge(ev("exps"), 1)
                steps(dve.tensor_reduce(SM[:, :, 1:2], PR[:, :, :], AX.X, ALU.add))
                steps.wait()
                steps(dve.reciprocal(SM[:, :, 1:2], SM[:, :, 1:2]))
                steps.wait()
                steps(tt(PR[:, :, :], PR[:, :, :], e3(SM[:, :, 1:2]), ALU.mult))
                steps.wait()
                steps(dve.tensor_copy(PW[:, :, :], PR[:, :, :]))
                steps.wait()
                rank = RANK[:, :].rearrange("p (a e) -> p a e", a=1).broadcast_to([P, G, NE])
                for k_ in range(2):
                    steps(dve.tensor_reduce(SM[:, :, 2:3], PW[:, :, :], AX.X, ALU.max))
                    steps.wait()
                    steps(tt(OH[:, :, :], PW[:, :, :], e3(SM[:, :, 2:3]), ALU.is_equal))
                    steps.wait()
                    steps(tt(OH[:, :, :], OH[:, :, :], rank, ALU.mult))
                    steps.wait()
                    steps(dve.tensor_reduce(SM[:, :, 3:4], OH[:, :, :], AX.X, ALU.max))
                    steps.wait()
                    steps(tt(OH[:, :, :], OH[:, :, :], e3(SM[:, :, 3:4]), ALU.is_equal))
                    steps.wait()
                    if k_ == 0:
                        steps(dve.tensor_copy(CMB[:, :, :], OH[:, :, :]))
                    else:
                        steps(tt(CMB[:, :, :], CMB[:, :, :], OH[:, :, :], ALU.add))
                    steps(stt(PW[:, :, :], OH[:, :, :], -2.0, PW[:, :, :], ALU.mult, ALU.add))
                    steps.wait()
                steps(tt(CMB[:, :, :], CMB[:, :, :], PR[:, :, :], ALU.mult))
                steps.wait()
                steps(dve.tensor_reduce(SM[:, :, 2:3], CMB[:, :, :], AX.X, ALU.add))
                steps.wait()
                steps(dve.reciprocal(SM[:, :, 2:3], SM[:, :, 2:3]))
                steps.wait()
                tt(CMB[:, :, :], CMB[:, :, :], e3(SM[:, :, 2:3]), ALU.mult).then_inc(ev("combine"), 1)
                dve.wait_ge(ev("combine"), 1)
                dve.wait_ge(ev("comb"), 1)

            def pair(l, i, e):
                n = number["gate", l, i, e]
                make_lo(n + 2)
                u = pair_no[l, i, e]
                k, w = tile_width(n)
                nb = w // P
                dve.wait_ge(act_read, read_no[n])
                if l % 2 == 1:
                    cb = CB[:, e:e + 1, :].broadcast_to([P, nb, TOK])
                    steps(tt(SL[:, u % 2, 0:nb, :], SL[:, u % 2, 0:nb, :], cb, ALU.mult))
                    steps.wait()
                dve.wait_ge(tile_done, n + 2)
                tt(SL[:, u % 2, 0:nb, :], SL[:, u % 2, 0:nb, :],
                   PS[:, bank_of[n + 1], 0:w * 2].rearrange("p (b t) -> p b t", t=TOK), ALU.mult).then_inc(ev("hidden"), 1)
                dve.wait_ge(ev("hidden"), u + 1)
                dve.sem_inc(dve_read, 1)
                make_lo(n + 3)
                dve.wait_ge(ev("pair_hi"), u + 1)
                o = (0 if l % 2 == 0 else 11 * (e % 2)) + 2 * i
                tt(AL[:, o:o + nb, :], SL[:, u % 2, 0:nb, :], AH[:, o:o + nb, :].bitcast(F32), ALU.subtract)\
                    .then_inc(ev("pair_lo"), 1)

            def down(l, e):
                for i in range(11 if l % 2 == 0 else 6):
                    if number["down", l, i, e] + 2 != behind_norm(2 * l + 1):
                        make_lo(number["down", l, i, e] + 2)

            k_bar = 0
            for item in sched:
                what, a = item[0], item[1:]
                if what == "barrier":
                    k_bar += 1
                    steps.wait()
                    dve.sem_inc(dve_stage, 1)
                    dve.wait_ge(act_stage, k_bar)
                elif what in ("in", "later"):
                    mixed(*a)
                elif what == "row":
                    make_lo(number["ada", a[0], a[1], 0] + 2)
                elif what in ("cond", "o", "part", "ada", "turn", "z"):
                    pass
                else:
                    {"bias": bias, "consts": consts, "params": params, "col": col, "keys": keys, "key_norms": key_norms,
                     "values": values, "ht": ht, "ht_done": ht_done, "wprep": wprep, "scan": scan,
                     "gn": gn, "sines": sines, "filter": filt, "conv": conv, "merge": merge, "gates": gates,
                     "resid": resid, "affine": affine, "router": router,
                     "pair": pair, "down": down}[what](*a)


def kernel(**inputs):
    import concourse.bacc as bacc
    from concourse.bass_utils import run_bass_kernel_spmd

    nc = bacc.Bacc("TRN2", target_bir_lowering=False, num_devices=1)
    arrays, aps = {}, {}
    for name, value in [*inputs.items(), *shape_constants().items()]:
        a = np.ascontiguousarray(value)
        arrays[f"in_{name}"] = a
        aps[name] = nc.dram_tensor(f"in_{name}", a.shape, mybir.dt.from_np(a.dtype), kind="ExternalInput").ap()
    outs = [nc.dram_tensor(f"out_{i}", shape, F32, kind="ExternalOutput").ap()
            for i, shape in enumerate([(1, T, D), (1, T, D), (1, LAYERS, 2, NH, HD, HD)])]
    build(nc, aps, *outs)
    r = run_bass_kernel_spmd(nc, [arrays], core_ids=[0])
    return tuple(r.results[0][f"out_{i}"] for i in range(3))
```
